# Optimizing a Trainium2 kernel written in Bass

```python
import jax, jax.numpy as jnp
from jax import lax
import numpy as np

D_MODEL = 2048
BATCH = 1
SEQ = 512
DEPTH = 1

N_MIXERS = 3
GRID_W = 64
BRANCH_W = D_MODEL
NORM_EPS = 1e-6

POOL_WINDOWS = (2, 4, 8, 16)
N_POOL_GROUPS = 4
POOL_GROUP_DIM = BRANCH_W // N_POOL_GROUPS

GLA_HEADS = 4
GLA_KEY_W = D_MODEL // 2
GLA_VAL_W = BRANCH_W
GLA_DK = GLA_KEY_W // GLA_HEADS
GLA_DV = GLA_VAL_W // GLA_HEADS
GLA_LOWRANK = 16
GLA_TAU = 16.0
GLA_CHUNK = 64

ATTN_HEAD_DIM = 128
ATTN_HEADS = BRANCH_W // ATTN_HEAD_DIM
ATTN_KV_HEADS = 4
ATTN_GROUP = ATTN_HEADS // ATTN_KV_HEADS
ATTN_Q_W = ATTN_HEADS * ATTN_HEAD_DIM
ATTN_KV_W = ATTN_KV_HEADS * ATTN_HEAD_DIM
ATTN_BLOCK = 128
ROPE_AXIS_DIM = ATTN_HEAD_DIM // 2
ROPE_THETA = 10000.0


def rms_norm(x, eps=NORM_EPS):
    xf = x.astype(jnp.float32)
    return (xf * lax.rsqrt(jnp.mean(xf * xf, axis=-1, keepdims=True) + eps)).astype(x.dtype)

def ada_modulation(c, w, b):
    m = jnp.dot(jax.nn.silu(c), w) + b
    shift, scale, gate = jnp.split(m, 3, axis=-1)
    return shift[:, None], scale[:, None], gate[:, None]

def centred_window_mean(u, w):
    T = u.shape[1]
    csum = jnp.cumsum(u.astype(jnp.float32), axis=1)
    P = jnp.concatenate([jnp.zeros_like(csum[:, :1]), csum], axis=1)
    t = jnp.arange(T)
    lo = jnp.maximum(t - w // 2, 0)
    hi = jnp.minimum(t + w // 2, T)
    cnt = (hi - lo).astype(jnp.float32)
    return ((P[:, hi] - P[:, lo]) / cnt[None, :, None]).astype(u.dtype)

def pool_mixer(h, w_in, w_grp, scale, w_out):
    B, T, _ = h.shape
    u, g = jnp.split(h @ w_in, 2, axis=-1)
    ug = u.reshape(B, T, N_POOL_GROUPS, POOL_GROUP_DIM)
    pooled = jnp.stack(
        [centred_window_mean(ug[:, :, i], w) - ug[:, :, i] for i, w in enumerate(POOL_WINDOWS)],
        axis=2)
    y = jnp.einsum('btgc,gcd->btgd', pooled, w_grp).reshape(B, T, BRANCH_W) * scale
    return (y * jax.nn.silu(g)) @ w_out

def gla_chunked_scan(q, k, v, log_a, include_diag):
    B, T, H, DK = q.shape
    DV = v.shape[-1]
    nc = T // GLA_CHUNK

    def to_chunks(z):
        return z.astype(jnp.float32).reshape(B, nc, GLA_CHUNK, H, z.shape[-1]).transpose(1, 0, 3, 2, 4)

    qc, kc, vc, ac = to_chunks(q), to_chunks(k), to_chunks(v), to_chunks(log_a)
    mask = jnp.tril(jnp.ones((GLA_CHUNK, GLA_CHUNK), dtype=bool), 0 if include_diag else -1)

    def step(S, inp):
        qi, ki, vi, ai = inp
        b = jnp.cumsum(ai, axis=2)
        o_inter = jnp.einsum('bhcd,bhde->bhce', qi * jnp.exp(b), S)
        diff = b[:, :, :, None, :] - b[:, :, None, :, :]
        decay = jnp.exp(jnp.where(mask[:, :, None], diff, -jnp.inf))
        A = jnp.sum(qi[:, :, :, None, :] * ki[:, :, None, :, :] * decay, axis=-1)
        o_intra = jnp.einsum('bhij,bhje->bhie', A, vi)
        b_last = b[:, :, -1:, :]
        S_new = jnp.exp(b_last[:, :, 0, :])[..., None] * S + jnp.einsum(
            'bhjd,bhje->bhde', ki * jnp.exp(b_last - b), vi)
        return S_new, o_inter + o_intra

    S0 = jnp.zeros((B, H, DK, DV), jnp.float32)
    _, o = lax.scan(step, S0, (qc, kc, vc, ac))
    return o.transpose(1, 0, 3, 2, 4).reshape(B, T, H, DV)

def gla_mixer(h, w_in, fwd_w1, fwd_w2, fwd_b, bwd_w1, bwd_w2, bwd_b, norm_g, w_out):
    B, T, _ = h.shape
    q, k, v, g = jnp.split(h @ w_in, [GLA_KEY_W, 2 * GLA_KEY_W, 2 * GLA_KEY_W + GLA_VAL_W], axis=-1)
    q = (q * GLA_DK ** -0.5).reshape(B, T, GLA_HEADS, GLA_DK)
    k = k.reshape(B, T, GLA_HEADS, GLA_DK)
    v = v.reshape(B, T, GLA_HEADS, GLA_DV)

    def log_decay(w1, w2, b):
        z = ((h @ w1) @ w2 + b).astype(jnp.float32)
        return (jax.nn.log_sigmoid(z) / GLA_TAU).reshape(B, T, GLA_HEADS, GLA_DK)

    rev = lambda z: z[:, ::-1]
    o_fwd = gla_chunked_scan(q, k, v, log_decay(fwd_w1, fwd_w2, fwd_b), include_diag=True)
    o_bwd = rev(gla_chunked_scan(rev(q), rev(k), rev(v), rev(log_decay(bwd_w1, bwd_w2, bwd_b)),
                                 include_diag=False))
    o = (rms_norm(o_fwd + o_bwd) * norm_g).reshape(B, T, GLA_VAL_W).astype(h.dtype)
    return (o * jax.nn.silu(g)) @ w_out

def axial_rope_tables(T):
    rows = T // GRID_W
    t = jnp.arange(T)
    row = (t // GRID_W - rows // 2).astype(jnp.float32)
    col = (t % GRID_W - GRID_W // 2).astype(jnp.float32)
    inv = ROPE_THETA ** (-jnp.arange(0, ROPE_AXIS_DIM, 2, dtype=jnp.float32) / ROPE_AXIS_DIM)
    ang = jnp.concatenate([row[:, None] * inv, col[:, None] * inv], axis=-1)
    return jnp.cos(ang), jnp.sin(ang)

def apply_rope(x, cos, sin):
    shp = (cos.shape[0],) + (1,) * (x.ndim - 3) + (cos.shape[1],)
    cos = cos.reshape(shp).astype(x.dtype)
    sin = sin.reshape(shp).astype(x.dtype)
    xr = x.reshape(x.shape[:-1] + (-1, 2))
    x0, x1 = xr[..., 0], xr[..., 1]
    return jnp.stack([x0 * cos - x1 * sin, x0 * sin + x1 * cos], axis=-1).reshape(x.shape)

def attn_mixer(h, w_in, q_norm_g, k_norm_g, w_out):
    B, T, _ = h.shape
    q, k, v, g = jnp.split(h @ w_in, [ATTN_Q_W, ATTN_Q_W + ATTN_KV_W, ATTN_Q_W + 2 * ATTN_KV_W], axis=-1)
    q = rms_norm(q.reshape(B, T, ATTN_KV_HEADS, ATTN_GROUP, ATTN_HEAD_DIM)) * q_norm_g
    k = rms_norm(k.reshape(B, T, ATTN_KV_HEADS, ATTN_HEAD_DIM)) * k_norm_g
    v = v.reshape(B, T, ATTN_KV_HEADS, ATTN_HEAD_DIM)
    cos, sin = axial_rope_tables(T)
    q = apply_rope(q, cos, sin) * ATTN_HEAD_DIM ** -0.5
    k = apply_rope(k, cos, sin)
    nb = T // ATTN_BLOCK
    qb = q.reshape(B, nb, ATTN_BLOCK, ATTN_KV_HEADS, ATTN_GROUP, ATTN_HEAD_DIM).transpose(1, 0, 2, 3, 4, 5)

    def block(qi):
        s = jnp.einsum('bqkgd,bskd->bkgqs', qi, k, preferred_element_type=jnp.float32)
        p = jax.nn.softmax(s, axis=-1).astype(v.dtype)
        return jnp.einsum('bkgqs,bskd->bqkgd', p, v)

    o = lax.map(block, qb).transpose(1, 0, 2, 3, 4, 5).reshape(B, T, ATTN_Q_W)
    return (o * jax.nn.silu(g)) @ w_out

def first_inputs(seed: int = 0) -> dict:
    key = jax.random.key(seed)
    ks = iter(jax.random.split(key, 40))
    n_pool = len(range(0, DEPTH, N_MIXERS))
    n_gla = len(range(1, DEPTH, N_MIXERS))
    n_attn = len(range(2, DEPTH, N_MIXERS))
    D = D_MODEL

    def nrm(shape, scale):
        return jax.random.normal(next(ks), shape, jnp.float32) * scale

    def gain(shape):
        return 1.0 + 0.1 * jax.random.normal(next(ks), shape, jnp.float32)

    return {
        "x": nrm((BATCH, SEQ, D), 1.0),
        "c": nrm((BATCH, D), 1.0),
        "w_mod": nrm((DEPTH, D, 3 * D), 0.5 * D ** -0.5),
        "b_mod": nrm((DEPTH, 3 * D), 0.02),
        "pool_w_in": nrm((n_pool, D, 2 * BRANCH_W), D ** -0.5),
        "pool_w_grp": nrm((n_pool, N_POOL_GROUPS, POOL_GROUP_DIM, POOL_GROUP_DIM), POOL_GROUP_DIM ** -0.5),
        "pool_scale": gain((n_pool, BRANCH_W)),
        "pool_w_out": nrm((n_pool, BRANCH_W, D), BRANCH_W ** -0.5),
        "gla_w_in": nrm((n_gla, D, 2 * GLA_KEY_W + 2 * GLA_VAL_W), D ** -0.5),
        "gla_fwd_w1": nrm((n_gla, D, GLA_LOWRANK), D ** -0.5),
        "gla_fwd_w2": nrm((n_gla, GLA_LOWRANK, GLA_KEY_W), GLA_LOWRANK ** -0.5),
        "gla_fwd_b": nrm((n_gla, GLA_KEY_W), 0.1),
        "gla_bwd_w1": nrm((n_gla, D, GLA_LOWRANK), D ** -0.5),
        "gla_bwd_w2": nrm((n_gla, GLA_LOWRANK, GLA_KEY_W), GLA_LOWRANK ** -0.5),
        "gla_bwd_b": nrm((n_gla, GLA_KEY_W), 0.1),
        "gla_norm_g": gain((n_gla, GLA_DV)),
        "gla_w_out": nrm((n_gla, GLA_VAL_W, D), GLA_VAL_W ** -0.5),
        "attn_w_in": nrm((n_attn, D, 2 * ATTN_Q_W + 2 * ATTN_KV_W), D ** -0.5),
        "attn_q_norm_g": gain((n_attn, ATTN_HEAD_DIM)),
        "attn_k_norm_g": gain((n_attn, ATTN_HEAD_DIM)),
        "attn_w_out": nrm((n_attn, ATTN_Q_W, D), ATTN_Q_W ** -0.5),
        "final_norm_g": gain((D,)),
    }

def first_block(x, c, w_mod, b_mod, pool_w_in, pool_w_grp, pool_scale, pool_w_out,
              gla_w_in, gla_fwd_w1, gla_fwd_w2, gla_fwd_b, gla_bwd_w1, gla_bwd_w2, gla_bwd_b,
              gla_norm_g, gla_w_out, attn_w_in, attn_q_norm_g, attn_k_norm_g, attn_w_out,
              final_norm_g):
    for i in range(DEPTH):
        shift, scale, gate = ada_modulation(c, w_mod[i], b_mod[i])
        h = rms_norm(x) * (1.0 + scale) + shift
        kind, j = i % N_MIXERS, i // N_MIXERS
        if kind == 0:
            y = pool_mixer(h, pool_w_in[j], pool_w_grp[j], pool_scale[j], pool_w_out[j])
        elif kind == 1:
            y = gla_mixer(h, gla_w_in[j], gla_fwd_w1[j], gla_fwd_w2[j], gla_fwd_b[j],
                          gla_bwd_w1[j], gla_bwd_w2[j], gla_bwd_b[j], gla_norm_g[j], gla_w_out[j])
        else:
            y = attn_mixer(h, attn_w_in[j], attn_q_norm_g[j], attn_k_norm_g[j], attn_w_out[j])
        x = x + gate * y
    return rms_norm(x) * final_norm_g


HEAD_DIM = 64
A_Q_HEADS = 12
A_KV_HEADS = 4
A_GROUP = A_Q_HEADS // A_KV_HEADS
WINDOW = 128
BLOCK = 128
B_HEADS = 12
C_HEADS = 4
C_HEAD_DIM = 128
MEM_TOKENS = 256
N_BRANCHES = 3
A_WIDTH = A_Q_HEADS * HEAD_DIM
A_KV_WIDTH = A_KV_HEADS * HEAD_DIM
B_WIDTH = B_HEADS * HEAD_DIM
C_WIDTH = C_HEADS * C_HEAD_DIM
EPS = 1e-6
NEG = -1e30

IN_SIZES = (A_WIDTH, A_KV_WIDTH, A_KV_WIDTH, A_WIDTH,
            B_WIDTH, B_WIDTH, B_WIDTH, B_WIDTH, B_HEADS,
            C_WIDTH, C_WIDTH,
            N_BRANCHES * D_MODEL)
IN_WIDTH = sum(IN_SIZES)
IN_OFFSETS = tuple(int(o) for o in np.cumsum(IN_SIZES)[:-1])


def rms_norm_2(x, gain):
    x32 = x.astype(jnp.float32)
    y = x32 * lax.rsqrt(jnp.mean(x32 * x32, axis=-1, keepdims=True) + EPS)
    return (y * gain.astype(jnp.float32)).astype(x.dtype)

def alibi_slopes(n_heads):
    h = jnp.arange(1, n_heads + 1, dtype=jnp.float32)
    return jnp.exp2(-8.0 * h / n_heads)

def sliding_window_attention(q, k, v, q_gain, k_gain, sinks):
    b, s, _, d = q.shape
    nb = s // BLOCK
    q = rms_norm_2(q, q_gain).astype(jnp.float32)
    k = rms_norm_2(k, k_gain).astype(jnp.float32)
    v = v.astype(jnp.float32)
    qb = q.reshape(b, nb, BLOCK, A_KV_HEADS, A_GROUP, d)
    pad = jnp.zeros((b, BLOCK, A_KV_HEADS, d), jnp.float32)
    kp = jnp.concatenate([pad, k], axis=1).reshape(b, nb + 1, BLOCK, A_KV_HEADS, d)
    vp = jnp.concatenate([pad, v], axis=1).reshape(b, nb + 1, BLOCK, A_KV_HEADS, d)
    kb = jnp.concatenate([kp[:, :-1], kp[:, 1:]], axis=2)
    vb = jnp.concatenate([vp[:, :-1], vp[:, 1:]], axis=2)
    scores = jnp.einsum('bnqkgd,bnskd->bnkgqs', qb, kb) * (d ** -0.5)
    qi = jnp.arange(BLOCK)[:, None]
    kj = jnp.arange(2 * BLOCK)[None, :]
    rel = qi + BLOCK - kj
    key_pos = jnp.arange(nb)[:, None, None] * BLOCK - BLOCK + kj[None]
    valid = (rel >= 0) & (rel < WINDOW) & (key_pos >= 0)
    slopes = alibi_slopes(A_Q_HEADS).reshape(A_KV_HEADS, A_GROUP)
    bias = -slopes[:, :, None, None] * rel.astype(jnp.float32)
    scores = jnp.where(valid[None, :, None, None], scores + bias[None, None], NEG)
    sink = sinks.astype(jnp.float32).reshape(A_KV_HEADS, A_GROUP)[None, None, :, :, None, None]
    m = jnp.maximum(jnp.max(scores, axis=-1, keepdims=True), sink)
    p = jnp.exp(scores - m)
    denom = jnp.sum(p, axis=-1, keepdims=True) + jnp.exp(sink - m)
    out = jnp.einsum('bnkgqs,bnskd->bnqkgd', p / denom, vb)
    return out.reshape(b, s, A_Q_HEADS * d)

def forgetting_attention(q, k, v, f_logit, q_gain, k_gain):
    b, s, h, d = q.shape
    nb = s // BLOCK
    q = rms_norm_2(q, q_gain).astype(jnp.float32)
    k = rms_norm_2(k, k_gain).astype(jnp.float32)
    v = v.astype(jnp.float32)
    log_f = jax.nn.log_sigmoid(f_logit.astype(jnp.float32))
    c = jnp.cumsum(log_f, axis=1).transpose(0, 2, 1)
    q_blocks = q.reshape(b, nb, BLOCK, h, d).transpose(1, 0, 2, 3, 4)
    cq_blocks = c.reshape(b, h, nb, BLOCK).transpose(2, 0, 1, 3)
    key_pos = jnp.arange(s)
    scale = d ** -0.5

    def block_fn(args):
        qb, cqb, n = args
        sc = jnp.einsum('bqhd,bshd->bhqs', qb, k) * scale + cqb[..., None] - c[:, :, None, :]
        qpos = n * BLOCK + jnp.arange(BLOCK)
        mask = key_pos[None, :] <= qpos[:, None]
        sc = jnp.where(mask[None, None], sc, NEG)
        p = jax.nn.softmax(sc, axis=-1)
        return jnp.einsum('bhqs,bshd->bqhd', p, v)

    out = lax.map(block_fn, (q_blocks, cq_blocks, jnp.arange(nb)))
    return out.transpose(1, 0, 2, 3, 4).reshape(b, s, h * d)

def memory_attention(q, mk, mv, q_gain, k_gain):
    b, s, h, d = q.shape
    q = rms_norm_2(q, q_gain).astype(jnp.float32)
    mk = rms_norm_2(mk, k_gain).astype(jnp.float32)
    sc = jnp.einsum('bthd,bmhd->bhtm', q, mk) * (d ** -0.5)
    p = jax.nn.softmax(sc, axis=-1)
    out = jnp.einsum('bhtm,bmhd->bthd', p, mv.astype(jnp.float32))
    return out.reshape(b, s, h * d)

def hybrid_layer(x, mem, norm_gain, mem_norm_gain, w_in, b_forget,
                 q_gain_a, k_gain_a, sinks_a, q_gain_b, k_gain_b, q_gain_c, k_gain_c,
                 w_mem_kv, w_branch_a, w_branch_b, w_branch_c, w_out):
    b, s, _ = x.shape
    hn = rms_norm_2(x, norm_gain)
    proj = hn @ w_in
    (qa, ka, va, za, qb, kb, vb, zb, fb, qc, zc, gate_logits) = jnp.split(proj, IN_OFFSETS, axis=-1)

    ya = sliding_window_attention(qa.reshape(b, s, A_Q_HEADS, HEAD_DIM),
                                  ka.reshape(b, s, A_KV_HEADS, HEAD_DIM),
                                  va.reshape(b, s, A_KV_HEADS, HEAD_DIM),
                                  q_gain_a, k_gain_a, sinks_a).astype(x.dtype)
    ua = (ya * jax.nn.silu(za)) @ w_branch_a

    yb = forgetting_attention(qb.reshape(b, s, B_HEADS, HEAD_DIM),
                              kb.reshape(b, s, B_HEADS, HEAD_DIM),
                              vb.reshape(b, s, B_HEADS, HEAD_DIM),
                              fb + b_forget, q_gain_b, k_gain_b).astype(x.dtype)
    ub = (yb * jax.nn.silu(zb)) @ w_branch_b

    mkv = rms_norm_2(mem, mem_norm_gain) @ w_mem_kv
    mk, mv = jnp.split(mkv, 2, axis=-1)
    mlen = mem.shape[1]
    yc = memory_attention(qc.reshape(b, s, C_HEADS, C_HEAD_DIM),
                          mk.reshape(b, mlen, C_HEADS, C_HEAD_DIM),
                          mv.reshape(b, mlen, C_HEADS, C_HEAD_DIM),
                          q_gain_c, k_gain_c).astype(x.dtype)
    uc = (yc * jax.nn.silu(zc)) @ w_branch_c

    g = jax.nn.sigmoid(gate_logits.reshape(b, s, N_BRANCHES, D_MODEL))
    y = g[:, :, 0] * ua + g[:, :, 1] * ub + g[:, :, 2] * uc
    return x + y @ w_out

def second_inputs(seed: int = 0) -> dict:
    key = jax.random.key(seed)
    ks = jax.random.split(key, 20)
    f32 = jnp.float32
    nrm = lambda k, shape: jax.random.normal(k, shape, f32)
    return {
        "x": nrm(ks[0], (BATCH, SEQ, D_MODEL)),
        "mem": nrm(ks[1], (BATCH, MEM_TOKENS, D_MODEL)),
        "norm_gain": 1.0 + 0.02 * nrm(ks[2], (DEPTH, D_MODEL)),
        "mem_norm_gain": 1.0 + 0.02 * nrm(ks[3], (DEPTH, D_MODEL)),
        "w_in": nrm(ks[4], (DEPTH, D_MODEL, IN_WIDTH)) * D_MODEL ** -0.5,
        "b_forget": 3.0 + 0.5 * nrm(ks[5], (DEPTH, B_HEADS)),
        "q_gain_a": 1.0 + 0.02 * nrm(ks[6], (DEPTH, HEAD_DIM)),
        "k_gain_a": 1.0 + 0.02 * nrm(ks[7], (DEPTH, HEAD_DIM)),
        "sinks_a": 0.5 * nrm(ks[8], (DEPTH, A_Q_HEADS)),
        "q_gain_b": 1.0 + 0.02 * nrm(ks[9], (DEPTH, HEAD_DIM)),
        "k_gain_b": 1.0 + 0.02 * nrm(ks[10], (DEPTH, HEAD_DIM)),
        "q_gain_c": 1.0 + 0.02 * nrm(ks[11], (DEPTH, C_HEAD_DIM)),
        "k_gain_c": 1.0 + 0.02 * nrm(ks[12], (DEPTH, C_HEAD_DIM)),
        "w_mem_kv": nrm(ks[13], (DEPTH, D_MODEL, 2 * C_WIDTH)) * D_MODEL ** -0.5,
        "w_branch_a": nrm(ks[14], (DEPTH, A_WIDTH, D_MODEL)) * A_WIDTH ** -0.5,
        "w_branch_b": nrm(ks[15], (DEPTH, B_WIDTH, D_MODEL)) * B_WIDTH ** -0.5,
        "w_branch_c": nrm(ks[16], (DEPTH, C_WIDTH, D_MODEL)) * C_WIDTH ** -0.5,
        "w_out": nrm(ks[17], (DEPTH, D_MODEL, D_MODEL)) * D_MODEL ** -0.5,
    }

def second_block(x, mem, norm_gain, mem_norm_gain, w_in, b_forget,
              q_gain_a, k_gain_a, sinks_a, q_gain_b, k_gain_b, q_gain_c, k_gain_c,
              w_mem_kv, w_branch_a, w_branch_b, w_branch_c, w_out):
    for layer in range(DEPTH):
        x = hybrid_layer(x, mem, norm_gain[layer], mem_norm_gain[layer], w_in[layer], b_forget[layer],
                         q_gain_a[layer], k_gain_a[layer], sinks_a[layer],
                         q_gain_b[layer], k_gain_b[layer], q_gain_c[layer], k_gain_c[layer],
                         w_mem_kv[layer], w_branch_a[layer], w_branch_b[layer], w_branch_c[layer],
                         w_out[layer])
    return x


def setup_inputs(seed=0):
    out = dict(first_inputs(seed))
    for name, value in second_inputs(seed + 1).items():
        if name != "x":
            out[name + "_2"] = value
    return out


def reference(
    x, c, w_mod, b_mod, pool_w_in, pool_w_grp, pool_scale, pool_w_out, gla_w_in, gla_fwd_w1,
    gla_fwd_w2, gla_fwd_b, gla_bwd_w1, gla_bwd_w2, gla_bwd_b, gla_norm_g, gla_w_out, attn_w_in,
    attn_q_norm_g, attn_k_norm_g, attn_w_out, final_norm_g, mem_2, norm_gain_2, mem_norm_gain_2,
    w_in_2, b_forget_2, q_gain_a_2, k_gain_a_2, sinks_a_2, q_gain_b_2, k_gain_b_2, q_gain_c_2,
    k_gain_c_2, w_mem_kv_2, w_branch_a_2, w_branch_b_2, w_branch_c_2, w_out_2,
):
    x = first_block(
        x, c, w_mod, b_mod, pool_w_in, pool_w_grp, pool_scale, pool_w_out, gla_w_in, gla_fwd_w1,
        gla_fwd_w2, gla_fwd_b, gla_bwd_w1, gla_bwd_w2, gla_bwd_b, gla_norm_g, gla_w_out,
        attn_w_in, attn_q_norm_g, attn_k_norm_g, attn_w_out, final_norm_g,
    )
    return second_block(
        x, mem_2, norm_gain_2, mem_norm_gain_2, w_in_2, b_forget_2, q_gain_a_2, k_gain_a_2,
        sinks_a_2, q_gain_b_2, k_gain_b_2, q_gain_c_2, k_gain_c_2, w_mem_kv_2, w_branch_a_2,
        w_branch_b_2, w_branch_c_2, w_out_2,
    )


_drawn_inputs = setup_inputs


def setup_inputs(seed=0):
    import zlib

    import numpy as np

    out = dict(_drawn_inputs(seed))
    spreads = {}
    factors = {'b_mod': 4.053,
     'pool_scale': 2.941,
     'norm_gain_2': 8.0,
     'mem_norm_gain_2': 8.0,
     'q_gain_a_2': 8.0,
     'k_gain_a_2': 8.0,
     'sinks_a_2': 200.0,
     'q_gain_b_2': 8.0,
     'k_gain_b_2': 8.0,
     'q_gain_c_2': 8.0,
     'k_gain_c_2': 8.0}
    for name, (base, spread) in spreads.items():
        noise = np.random.default_rng([zlib.crc32(name.encode()), seed]).standard_normal(out[name].shape)
        drawn = base * np.exp(spread * noise) if base else spread * noise
        out[name] = __import__('jax').numpy.asarray(drawn.astype(out[name].dtype))
    for name, factor in factors.items():
        out[name] = (out[name] * factor).astype(out[name].dtype)
    return out
```

```python
from contextlib import ExitStack, contextmanager

import numpy as np
import concourse.bass as bass
from concourse import mybir

F32 = mybir.dt.float32
F32R = mybir.dt.float32r
BF16 = mybir.dt.bfloat16
ACT = mybir.ActivationFunctionType
ALU = mybir.AluOpType

P = 128
D = 2048
T = 512
KT = D // P
NB = T // P
MEM = 256
POOL_WINDOWS = (2, 4, 8, 16)
PAD = POOL_WINDOWS[-1] // 2
ROW = T + 2 * PAD
HEAD = 64
GROUPS = 3
HEADS_A, HEADS_B, HEADS_C = 12, 12, 4
EPS = 1e-6
NEG = -1e30
FAR = -1e36

STAGES = [("mem", 2 * HEADS_C), ("pool_in", 2 * KT), ("group", 4), ("pool_out", KT), ("forget", 1),
          ("b", 4 * HEADS_B // 2), ("a", 2 * (2 + 2 * GROUPS)), ("c", 2 * HEADS_C),
          ("gated", 4 * KT), ("out", KT)]
FIRST = {}
_n = 0
for _name, _count in STAGES:
    FIRST[_name] = _n
    _n += _count
PANELS = _n
RESULT = {"mem": 0, "pool_in": 8, "group": 40, "pool_out": 56, "forget": 72, "b": 73, "a": 97, "c": 113,
          "gated": 121, "out": 217}

COLS = {}
_n = 0
for _name, _count in [("b_mod", 3 * KT), ("pool_scale", KT), ("final_g", KT), ("norm_g", KT), ("mem_g", KT),
                      ("b_forget", 1), ("qg_a", 1), ("kg_a", 1), ("qg_b", 1), ("kg_b", 1), ("qg_c", 1),
                      ("kg_c", 1), ("sinks", HEADS_A)]:
    COLS[_name] = (_n, _n + _count)
    _n += _count
NCOLS = _n
CONST = {}
_n = 0
for _name, _count in [("ident", P), ("ones", P), ("blocks", P), ("causal", P), ("edges", 4 * 2 * PAD),
                      ("slopes", HEADS_A)]:
    CONST[_name] = (_n, _n + _count)
    _n += _count
NCONST = _n


def a_heads():
    return [GROUPS * (2 * c + hh) + g for c in range(2) for g in range(GROUPS) for hh in range(2)]


class Step:

    def __init__(self, register, first):
        self.register, self.first = register, first


@contextmanager
def steps(eng, first, end):
    with eng.Fori(first, end) as register:
        yield Step(register, first)


class At:

    def __init__(self, c, k=0, i=None):
        self.c, self.k, self.i = c, k, i

    def __add__(self, n):
        return At(self.c + n, self.k, self.i)

    def __sub__(self, n):
        return At(self.c - n, self.k, self.i)

    def times(self, m):
        return At(self.c * m, self.k * m, self.i)

    def half(self):
        assert self.k % 2 == 0
        return At(self.c // 2, self.k // 2, self.i)

    def parity(self):
        assert self.k % 2 == 0
        return self.c % 2

    def value(self):
        return self.c if self.i is None else self.i.register * self.k + self.c

    def lowest(self):
        return self.c if self.i is None else self.i.first * self.k + self.c

    def positive(self):
        assert self.i is None or self.lowest() > 0
        return self.lowest() > 0

    def pick(self, size=1):
        return slice(self.c, self.c + size) if self.i is None else bass.ds(self.value(), size)


ONE = 1


def program(nc, stream, wmod, cvec, xT, memT, cols_in, const_in, dist_in, x_store, c_store, mkv_store, out):
    ctx = ExitStack()
    with ctx:
        def sem(name):
            return ctx.enter_context(nc.semaphore(name))

        KB = 1024
        top = [16512]

        def region(size):
            at = top[0]
            top[0] += size
            assert top[0] <= 229344, top[0]
            return at

        def sb(name, shape, dt, at):
            return nc.alloc_sbuf_tensor_at(name, shape, dt, offset=at)

        at_w = region(24 * KB)
        at_x1, at_x2, at_x3 = region(64 * KB), region(64 * KB), region(32 * KB)
        at_const = region(3712)
        at_scratch = region(20 * KB)

        w_raw = sb("w_raw", [P, 2, 8 * P], F32, at_w)
        w_hi = sb("w_hi", [P, 4, 4 * P], F32R, at_w + 8 * KB)
        w_lo = sb("w_lo", [P, 4, 4 * P], F32R, at_w + 16 * KB)
        x1_hi = sb("x1_hi", [P, KT, T], F32R, at_x1)
        x1_lo = sb("x1_lo", [P, KT, T], F32R, at_x1 + 32 * KB)
        x2_hi = sb("x2_hi", [P, KT, T], F32R, at_x2)
        x2_lo = sb("x2_lo", [P, KT, T], F32R, at_x2 + 32 * KB)
        x3 = sb("x3", [P, KT, T], F32, at_x3)

        cat = [at_const]

        def keep(name, shape, dt, size):
            at = cat[0]
            cat[0] += (size + 31) // 32 * 32
            assert cat[0] <= at_scratch
            return sb(name, shape, dt, at)

        ident = keep("ident", [P, P], F32, 512)
        ones = keep("ones", [P, P], F32, 512)
        blocks = keep("blocks", [P, P], F32, 512)
        edges = keep("edges", [P, 4, 2 * PAD], F32, 256)
        slopes = keep("slopes", [P, HEADS_A], F32, 48)
        ident_b = keep("ident_b", [P, P], BF16, 256)
        causal_b = keep("causal_b", [P, P], BF16, 256)
        cols = keep("cols", [P, NCOLS], F32, 4 * NCOLS)
        mod = keep("mod", [P, 3 * KT], F32, 4 * 3 * KT)
        hn_g = keep("hn_g", [P, KT], F32, 4 * KT)
        mod_part = keep("mod_part", [P, 4], F32, 16)
        neg_max = keep("neg_max", [P, 8], F32, 32)
        den = keep("den", [P, 8], F32, 32)
        rden = keep("rden", [P, 8], F32, 32)
        sink_exp = keep("sink_exp", [P, 8], F32, 32)
        sink_col = keep("sink_col", [P, 2], F32, 8)
        neg_sink = keep("neg_sink", [P, 2], F32, 8)
        arrived = keep("arrived", [P, 8], F32, 32)

        def col(name, n=None):
            a, b = COLS[name]
            if n is None:
                return cols[:, a:b]
            return cols[:, (n + a).pick()] if isinstance(n, At) else cols[:, a + n:a + n + 1]

        tmp = sb("tmp", [P, 2, T], F32, at_scratch)
        var = sb("var", [P, T], F32, at_scratch + 4 * KB)
        rs = sb("rs", [P, T], F32, at_scratch + 6 * KB)
        rs_sq = sb("rs_sq", [P, T], F32, at_scratch + 8 * KB)
        c_rows = sb("c_rows", [P, D], F32, at_scratch + 12 * KB)
        mem_out = sb("mem_out", [P, MEM], F32, at_scratch + 10 * KB)
        msrc0 = sb("msrc0", [P, MEM], F32, at_scratch + 11 * KB)
        urow = sb("urow", [P, ROW], F32, at_scratch + 10 * KB)
        wsum = [sb(f"wsum{n}", [P, ROW], F32, at_scratch + 10 * KB + (n + 1) * 4 * ROW) for n in range(2)]
        sig0 = sb("sig0", [P, T], F32, at_scratch + 10 * KB + 3 * 4 * ROW)
        x_in = sb("x_in", [P, 2, T], F32, at_scratch + 4 * KB)
        sq_a = sb("sq_a", [P, T], F32, at_scratch + 10 * KB)
        sq_b = sb("sq_b", [P, T], F32, at_scratch + 12 * KB)
        sum_a = sb("sum_a", [P, T], F32, at_scratch + 14 * KB)
        sum_b = sb("sum_b", [P, T], F32, at_scratch + 16 * KB)
        r_both = sb("r_both", [P, T], F32, at_scratch + 10 * KB)
        r_one = sb("r_one", [P, T], F32, at_scratch + 18 * KB)
        gate_sig = sb("gate_sig", [P, 3, T], F32, at_scratch + 10 * KB)
        part = sb("part", [P, 2, T], F32, at_scratch + 4 * KB)
        x_back = sb("x_back", [P, 2, T], F32, at_scratch + 10 * KB)
        result = sb("result", [P, 2, T], F32, at_scratch + 14 * KB)

        memn_hi = x2_hi[:, KT // 2:, :].rearrange("p a (b t) -> p (a b) t", b=2)
        memn_lo = x2_lo[:, :KT // 2, :].rearrange("p a (b t) -> p (a b) t", b=2)
        wmod_sb = [sb(f"wmod{n}", [P, D], F32, at_x2 + at * KB) for n, at in enumerate((0, 8, 48, 56))]
        c_rows3 = sb("c_rows3", [P, D], F32, at_x2 + 32 * KB)
        mem_raw = sb("mem_raw", [P, KT, MEM], F32, at_x1 + 48 * KB)
        squares = sb("squares", [P, 2, T], F32, at_x1)
        q_t = sb("q_t", [P, T], F32, at_x2)
        k_t = sb("k_t", [P, T], F32, at_x2 + 2 * KB)
        v_n = sb("v_n", [P, NB, P], F32, at_x2 + 4 * KB)
        z_exp = sb("z_exp", [P, T], F32, at_x2 + 6 * KB)
        z_t = sb("z_t", [P, T], F32, at_x2 + 8 * KB)
        msrc = sb("msrc", [P, T], F32, at_x2 + 10 * KB)
        probs = sb("probs", [P, 2, 10 * P], F32, at_x2 + 12 * KB)
        probs_t = sb("probs_t", [P, 2, 10 * P], F32, at_x2 + 22 * KB)
        neg_c = sb("neg_c", [P, 2, T], F32, at_x2 + 32 * KB)
        bias_a = sb("bias_a", [P, 2, 2 * P], F32, at_x2 + 36 * KB)
        dist_a = sb("dist_a", [P, 2 * P], F32, at_x2 + 38 * KB)
        zero_c = sb("zero_c", [P, MEM], F32, at_x2 + 39 * KB)
        plain = sb("plain", [P, T], F32, at_x2 + 46 * KB)
        f_a = sb("f_a", [P, T], F32, at_x2 + 40 * KB)
        f_b = sb("f_b", [P, T], F32, at_x2 + 42 * KB)
        f_c = sb("f_c", [P, T], F32, at_x2 + 44 * KB)

        bank = [ctx.enter_context(nc.psum_tensor(f"bank{n}", [P, T], F32)) for n in range(8)]
        acc = bank[0:2]
        score = bank[2:4]
        turned = bank[4:6]
        ctx_out = bank[6]
        misc = bank[7]

        consts_loaded, cols_loaded, mask_loaded = sem("consts_loaded"), sem("cols_loaded"), sem("mask_loaded")
        mem_loaded, x_loaded, c_loaded, dist_loaded = sem("mem_loaded"), sem("x_loaded"), sem("c_loaded"), sem("dist_loaded")
        consts_ready, c_ready = sem("consts_ready"), sem("c_silu_ready")
        w_loaded = [sem(f"w_half{n}_loaded") for n in range(2)]
        hi_ready, lo_ready, w_used = sem("w_hi_ready"), sem("w_lo_ready"), sem("w_quarter_used")
        wmod_loaded, wmod_used = [sem(f"wmod{n}_loaded") for n in range(4)], sem("wmod_used")
        square_ready, square_used = sem("square_ready"), sem("square_used")
        var_ready, rs_ready = sem("var_ready"), sem("rs_ready")
        rx_ready, xr_ready = sem("rx_ready"), sem("xr_ready")
        memn_ready, h_ready = sem("memn_ready"), sem("h_ready")
        acc_free = [sem(f"acc{n}_free") for n in range(2)]
        msrc_ready, misc_full, misc_free = sem("msrc_ready"), sem("misc_full"), sem("misc_free")
        mem_out_ready, mem_out_stored = sem("mem_out_ready"), sem("mem_out_stored")
        urow_zeroed, urow_ready, urow_used = sem("urow_zeroed"), sem("urow_ready"), sem("urow_used")
        sig_ready, sig_used = sem("sig_ready"), sem("sig_used")
        pooled_ready, yg_ready = sem("pooled_ready"), sem("yg_ready")
        x_in_loaded, gate_c_loaded = [sem(f"x_in{n}_loaded") for n in range(2)], sem("gate_c_loaded")
        x1_ready, sq_ready, sq_added = sem("x1_ready"), sem("square_pair_ready"), sem("square_pair_added")
        sums_zeroed, sums_full = sem("sums_zeroed"), sem("sums_full")
        hn_ready, xp_ready = sem("hn_ready"), sem("x_prime_ready")
        xp_stored = [sem(f"x_prime{n}_stored") for n in range(2)]
        f_abs, f_ln, c_neg_ready, c_stored = sem("f_abs_ready"), sem("f_ln_ready"), sem("c_neg_ready"), sem("c_stored")
        neg_c_loaded = [sem(f"neg_c{n}_loaded") for n in range(2)]
        k_loaded, v_loaded = sem("k_loaded"), sem("v_loaded")
        q_ready, k_ready, v_ready = sem("q_ready"), sem("k_ready"), sem("v_ready")
        plain_ready, plain_used = sem("plain_ready"), sem("plain_used")
        z_exp_ready, z_ready = sem("z_exp_ready"), sem("z_ready")
        score_full, score_read = sem("score_full"), sem("score_read")
        exp_done, sink_done, rden_ready = sem("exp_done"), sem("sink_exp_done"), sem("rden_ready")
        probs_ready, turned_full, turned_copied = sem("probs_ready"), sem("turned_full"), sem("turned_copied")
        pv_done, ctx_free = sem("pv_done"), sem("ctx_free")
        yz_ready, gsig_ready, branch_part = sem("yz_split"), sem("gate_sig_ready"), sem("branch_part")
        y_ready, y_split = sem("y_ready"), sem("y_split")
        x_back_loaded = [sem(f"x_back{n}_loaded") for n in range(2)]
        result_ready, result_stored = sem("result_ready"), [sem(f"result{n}_stored") for n in range(2)]

        from_one = [*acc_free, ctx_free, misc_free, misc_full, pv_done, *result_stored,
                       score_read, sig_used, sq_added, turned_copied]

        TOTAL = 4 * PANELS

        def load_panel(sp, g):
            srcs = [stream[g.pick(), :, half * 8 * P:(half + 1) * 8 * P].rearrange("a p n -> p (a n)") for half in range(2)]
            for half, src in enumerate(srcs):
                if ((g - 1).times(4) + (2 * half + 2)).positive():
                    sp.wait_ge(lo_ready, ((g - 1).times(4) + (2 * half + 2)).value())
                sp.dma_start(w_raw[:, half, :], src).then_inc(w_loaded[half], 16)

        def raw_quarter(q):
            return w_raw[:, q // 2, (q % 2) * 4 * P:(q % 2 + 1) * 4 * P]

        def split_hi(act, t):
            s = t + 3
            act.drain()
            if s.i is None and s.c >= TOTAL:
                return
            q = s.c % 4
            g = At(s.c // 4, s.k // 4, s.i)
            act.wait_ge(w_loaded[q // 2], (g + 1).times(16).value())
            if (s - 3).positive():
                act.wait_ge(w_used, (s - 3).value())
            nc.scalar.activation(w_hi[:, q, :], raw_quarter(q), ACT.Copy).then_inc(hi_ready, 1)

        def split_lo(dve, t):
            s = t + 3
            dve.drain()
            if s.i is None and s.c >= TOTAL:
                return
            q = s.c % 4
            dve.wait_ge(hi_ready, (s + 1).value())
            nc.vector.tensor_tensor(w_lo[:, q, :], raw_quarter(q), w_hi[:, q, :].bitcast(F32),
                                    ALU.subtract).then_inc(lo_ready, 1)

        def tile_products(bank_ap, q, k, x_hi, x_lo, kx, start, stop, tokens=T):
            hi, lo = w_hi[:, q, k * P:(k + 1) * P], w_lo[:, q, k * P:(k + 1) * P]
            nc.tensor.matmul(bank_ap[:, :tokens], hi, x_hi[:, kx, :], start=start, stop=False)
            nc.tensor.matmul(bank_ap[:, :tokens], hi, x_lo[:, kx, :], start=False, stop=False)
            return nc.tensor.matmul(bank_ap[:, :tokens], lo, x_hi[:, kx, :], start=False, stop=stop)

        def panel(pe, g, r, x_hi, x_lo, between=None, tokens=T, ready=None):
            pe.wait_ge(acc_free[r.parity()], (r.half() + ONE).value())
            for q in range(4):
                if between and q in between:
                    between[q]()
                if ready is not None:
                    pe.wait_ge(ready, 4 * (q + 1))
                t = g.times(4) + q
                pe.wait_ge(lo_ready, (t + 1).value())
                for k in range(4):
                    mm = tile_products(acc[r.parity()], q, k, x_hi, x_lo, 4 * q + k, q == 0 and k == 0,
                                       q == 3 and k == 3, tokens)
                mm.then_inc(w_used, 1)

        def rstd_guess(act, width, m):
            act.wait_ge(var_ready, (m + 1).value())
            nc.scalar.activation(rs[:, :width], var[:, :width], ACT.Ln)
            act.drain()
            nc.scalar.activation(rs[:, :width], rs[:, :width], ACT.Exp, scale=-0.5)
            act.drain()
            nc.scalar.activation(rs_sq[:, :width], rs[:, :width], ACT.Square).then_inc(rs_ready, 1)

        def rstd_newton(dve, dst, width, m):
            dve.wait_ge(rs_ready, (m + 1).value())
            nc.vector.scalar_tensor_tensor(rs_sq[:, :width], rs_sq[:, :width], -0.5, var[:, :width], ALU.mult, ALU.mult)
            dve.drain()
            nc.vector.scalar_tensor_tensor(dst, rs_sq[:, :width], 1.5, rs[:, :width], ALU.add, ALU.mult)
            dve.drain()

        def split_act(dve, src, hi, lo, ready):
            dve.drain()
            nc.vector.tensor_copy(hi, src)
            dve.drain()
            nc.vector.tensor_tensor(lo, src, hi.bitcast(F32), ALU.subtract).then_inc(ready, 1)
            dve.drain()

        def tile(x, n):
            return x[:, n.pick(), :].rearrange("p a t -> p (a t)")

        LEN = {"b": [P * (n + 1) for n in range(NB)], "a": [P] + [2 * P] * (NB - 1), "c": [MEM] * NB}
        KEY0 = {"b": [0] * NB, "a": [0] + [P * n for n in range(NB - 1)], "c": [0] * NB}
        OFF = {kind: [sum(LEN[kind][:n]) for n in range(NB)] for kind in LEN}

        def rows_of(kind, slot):
            return slice(0, P) if kind == "c" else slice(HEAD * slot, HEAD * slot + HEAD)

        class Attention:

            def __init__(self, kind, job, keys):
                self.kind, self.job, self.keys = kind, job, keys
                self.heads = 1 if kind == "c" else 2
                self.head = At(job.c + 12, job.k, job.i) if kind == "c" else job.times(2)
                self.done = self.head + self.heads
                self.tile = job + {"a": -6, "b": 6, "c": 0}[kind]

        class Window:

            def __init__(self, g, r, first, prev=None, prev_n=None, misc_n=None, rs_n=None, out_n=None,
                         attention=None, biased=None, loads=None, extra=None, scale=None):
                self.g, self.r, self.t = g, r, g.times(4)
                self.first, self.prev, self.prev_n = first, prev, prev_n
                self.misc_n, self.rs_n, self.out_n = misc_n, rs_n, out_n
                self.attention, self.biased, self.loads, self.extra, self.scale = attention, biased, loads, extra, scale

        def pe_scores(pe, at, slot):
            rows, head = rows_of(at.kind, slot), at.head + slot
            if slot == 0:
                pe.wait_ge(q_ready, (at.job + 1).value())
                if at.kind == "c":
                    pe.wait_ge(k_loaded, (at.keys.times(16)).value())
                else:
                    pe.wait_ge(k_ready, at.keys.value())
            for n in range(NB):
                pe.wait_ge(score_read, (head.times(4) + n + ONE).value())
                width, k0 = LEN[at.kind][n], KEY0[at.kind][n]
                mm = nc.tensor.matmul(score[n % 2][:, :width], q_t[rows, n * P:(n + 1) * P],
                                      k_t[rows, k0:k0 + width], start=True, stop=True)
                if at.kind == "b":
                    mm = nc.tensor.matmul(score[n % 2][:, width - P:width], ident_b[:, :], causal_b[:, :],
                                          start=False, stop=True, skip_group_check=True)
                mm.then_inc(score_full, 1)

        def pe_turn(pe, at, slot):
            head = at.head + slot
            for n in range(NB):
                pe.wait_ge(probs_ready, (head.times(4) + (n + 1)).value())
                pe.wait_ge(turned_copied, (head.times(4) + n + ONE).value())
                for kb in range(LEN[at.kind][n] // P):
                    o = OFF[at.kind][n] + kb * P
                    mm = nc.tensor.transpose(turned[n % 2][:, kb * P:(kb + 1) * P], probs[:, slot, o:o + P], ident[:, :])
                mm.then_inc(turned_full, 1)

        def pe_values(pe, at, slot):
            rows, head = rows_of(at.kind, slot), at.head + slot
            if slot == 0:
                pe.wait_ge(ctx_free, (at.job + ONE).value())
                if at.kind == "c":
                    pe.wait_ge(v_loaded, (at.keys.times(16)).value())
                else:
                    pe.wait_ge(v_ready, at.keys.value())
            for n in range(NB):
                pe.wait_ge(turned_copied, (head.times(4) + (n + 2) + ONE).value())
                count = LEN[at.kind][n] // P
                for kb in range(count):
                    o = OFF[at.kind][n] + kb * P
                    mm = nc.tensor.matmul(ctx_out[rows, n * P:(n + 1) * P], v_n[:, KEY0[at.kind][n] // P + kb, rows],
                                          probs_t[:, slot, o:o + P], start=kb == 0, stop=kb == count - 1)
            mm.then_inc(pv_done, 1)

        def pe_squares(pe, source, weights, width, m):
            pe.wait_ge(msrc_ready, (m + 1).value())
            pe.wait_ge(misc_free, (m + ONE).value())
            nc.tensor.matmul(misc[:, :width], weights[:, :], source[:, :width], start=True, stop=True).then_inc(misc_full, 1)

        def pe_turn_values(pe, source, width, m):
            pe.wait_ge(msrc_ready, (m + 1).value())
            pe.wait_ge(misc_free, (m + ONE).value())
            for kb in range(width // P):
                mm = nc.tensor.transpose(misc[:, kb * P:(kb + 1) * P], source[:, kb * P:(kb + 1) * P], ident[:, :])
            mm.then_inc(misc_full, 1)

        def pe_window(pe, w):
            at = w.attention
            two = at is not None and at.heads == 2

            def scores0():
                if at:
                    pe_scores(pe, at, 0)

            def values_of_prev():
                if w.prev == "v":
                    pe_turn_values(pe, msrc, T, w.misc_n)

            def scores1():
                if two:
                    pe_scores(pe, at, 1)

            def turn0():
                if at:
                    pe_turn(pe, at, 0)

            def values0():
                if at:
                    pe_values(pe, at, 0)
                if w.first != "gate":
                    pe_squares(pe, msrc, ones if w.first == "qc" else blocks, T, w.misc_n + (w.prev == "v"))

            def turn1():
                if two:
                    pe_turn(pe, at, 1)

            panel(pe, w.g, w.r, x1_hi, x1_lo, {1: scores0, 2: values_of_prev, 3: scores1})
            panel(pe, w.g + 1, w.r + 1, x1_hi, x1_lo, {1: turn0, 2: values0, 3: turn1})
            if two:
                pe_values(pe, at, 1)

        def act_exp(act, at, slot):
            head = at.head + slot
            for n in range(NB):
                c = 4 * slot + n
                act.wait_ge(score_read, (head.times(4) + (n + 2) + ONE).value())
                seg = probs[:, slot, OFF[at.kind][n]:OFF[at.kind][n] + LEN[at.kind][n]]
                nc.scalar.activation(seg, seg, ACT.Exp, bias=neg_max[:, c:c + 1], scale=-1.0,
                                     accum_out=den[:, c:c + 1]).then_inc(exp_done, 1)
            if at.kind == "a":
                nc.scalar.activation(sink_exp[:, 4 * slot:4 * slot + 4], neg_max[:, 4 * slot:4 * slot + 4], ACT.Exp,
                                     bias=sink_col[:, slot:slot + 1]).then_inc(sink_done, 1)

        def act_turned(act, at, slot):
            head = at.head + slot
            act.wait_ge(pv_done, (at.head + ONE).value())
            for n in range(NB):
                act.wait_ge(turned_full, (head.times(4) + (n + 1)).value())
                o, width = OFF[at.kind][n], LEN[at.kind][n]
                nc.scalar.activation(probs_t[:, slot, o:o + width], turned[n % 2][:, :width], ACT.Copy).then_inc(turned_copied, 1)

        def act_window(act, w):
            at = w.attention
            two = at is not None and at.heads == 2
            for s in range(8):
                t = w.t + s
                split_hi(act, t)
                if s == 0 and w.prev == "v":
                    act.wait_ge(w_used, t.value())
                    act.wait_ge(misc_full, (w.misc_n + ONE).value())
                    nc.scalar.activation(msrc[:, :], acc[(w.r - 1).parity()][:, :], ACT.Copy).then_inc(msrc_ready, 1)
                    act.drain().then_inc(acc_free[(w.r - 1).parity()], 1)
                if s == 0 and w.prev == "z":
                    act.wait_ge(w_used, t.value())
                    act.wait_ge(ctx_free, (w.prev_n + ONE).value())
                    before = acc[(w.r - 1).parity()]
                    nc.scalar.activation(z_exp[:, :], before[:, :], ACT.Exp, scale=-1.0)
                    nc.scalar.activation(z_t[:, :], before[:, :], ACT.Copy).then_inc(z_exp_ready, 1)
                    act.drain().then_inc(acc_free[(w.r - 1).parity()], 1)
                if s == 1 and w.prev == "f":
                    act.wait_ge(f_abs, 1)
                    nc.scalar.activation(f_c[:, :], f_b[:, :], ACT.Exp, scale=-1.0)
                    act.drain()
                    nc.scalar.activation(f_c[:, :], f_c[:, :], ACT.Ln, bias=1.0).then_inc(f_ln, 1)
                if s == 1 and at:
                    act_exp(act, at, 0)
                if s == 3 and two:
                    act_exp(act, at, 1)
                if s == 4 and w.first != "gate":
                    act.wait_ge(w_used, t.value())
                    act.wait_ge(misc_full, (w.misc_n + (w.prev == "v") + ONE).value())
                    if (w.rs_n - 8).positive():
                        act.wait_ge(plain_used, (w.rs_n - 8).value())
                    nc.scalar.activation(msrc[:, :], acc[w.r.parity()][:, :], ACT.Square).then_inc(msrc_ready, 1)
                    nc.scalar.activation(plain[:, :], acc[w.r.parity()][:, :], ACT.Copy).then_inc(plain_ready, 1)
                    act.drain().then_inc(acc_free[w.r.parity()], 1)
                if s == 4 and w.first == "gate":
                    act_gate(act, w.r, t, 0, w.out_n)
                if s == 5 and at:
                    act_turned(act, at, 0)
                if s == 6 and w.first != "gate":
                    rstd_guess(act, T, w.rs_n)
                if s == 7 and two:
                    act_turned(act, at, 1)

        def act_gate(act, r, t, b, n):
            act.wait_ge(w_used, t.value())
            if n.positive():
                act.wait_ge(y_ready, n.value())
            nc.scalar.activation(gate_sig[:, b, :], acc[r.parity()][:, :], ACT.Sigmoid).then_inc(gsig_ready, 1)
            act.drain().then_inc(acc_free[r.parity()], 1)

        def dve_scores(dve, at, slot):
            head = at.head + slot
            dve.drain()
            if at.kind == "b":
                dve.wait_ge(neg_c_loaded[slot], (at.job + 1).times(16).value())
            for n in range(NB):
                width = LEN[at.kind][n]
                dve.wait_ge(score_full, (head.times(4) + (n + 1)).value())
                if at.kind == "a":
                    bias, most = bias_a[:, slot, 2 * P - width:], neg_sink[:, slot:slot + 1]
                else:
                    bias, most = (neg_c[:, slot, :width] if at.kind == "b" else zero_c[:, :]), 3e38
                c = 4 * slot + n
                nc.vector.memset(arrived[:, c:c + 1], 0.0)
                nc.vector.tensor_tensor_reduce(
                    out=probs[:, slot, OFF[at.kind][n]:OFF[at.kind][n] + width], in0=score[n % 2][:, :width], in1=bias,
                    scale=-1.0, scalar=most, op0=ALU.add, op1=ALU.min, accum_out=neg_max[:, c:c + 1]).then_inc(score_read, 1)

        def dve_denominator(dve, at, slot):
            head = at.head + slot
            dve.wait_ge(exp_done, (head.times(4) + 4).value())
            seg = slice(4 * slot, 4 * slot + 4)
            if at.kind == "a":
                dve.wait_ge(sink_done, (head - 11).value())
                nc.vector.tensor_tensor(den[:, seg], den[:, seg], sink_exp[:, seg], ALU.add)
                dve.drain()
            nc.vector.reciprocal(rden[:, seg], den[:, seg]).then_inc(rden_ready, 1)

        def dve_window(dve, w):
            at = w.attention
            two = at is not None and at.heads == 2
            before = acc[(w.r - 1).parity()]
            for s in range(8):
                t = w.t + s
                split_lo(dve, t)
                if w.extra:
                    w.extra(s)
                if s == 0 and w.prev == "f":
                    dve.wait_ge(w_used, t.value())
                    nc.vector.tensor_scalar(f_a[:, :], before[:, :], col("b_forget"), None, ALU.add)
                    dve.drain().then_inc(acc_free[(w.r - 1).parity()], 1)
                    nc.vector.scalar_tensor_tensor(f_b[:, :], f_a[:, :], -1.0, f_a[:, :], ALU.mult, ALU.max).then_inc(f_abs, 1)
                if s == 2 and w.prev == "f":
                    dve.wait_ge(f_ln, 1)
                    nc.vector.tensor_scalar(f_a[:, :], f_a[:, :], 0.0, None, ALU.min)
                    dve.drain()
                    nc.vector.tensor_tensor(f_b[:, :], f_c[:, :], f_a[:, :], ALU.subtract)
                    dve.drain()
                if 3 <= s < 6 and w.prev == "f":
                    for step in range(3 * (s - 3), 3 * (s - 2)):
                        a, b = (f_b, f_a) if step % 2 == 0 else (f_a, f_b)
                        n = 1 << step
                        nc.vector.tensor_copy(b[:HEADS_B, :n], a[:HEADS_B, :n])
                        ins = nc.vector.tensor_tensor(b[:HEADS_B, n:], a[:HEADS_B, n:], a[:HEADS_B, :T - n], ALU.add)
                        if n == T // 2:
                            ins.then_inc(c_neg_ready, 1)
                        dve.drain()
                if s == 1 and at:
                    dve_scores(dve, at, 0)
                if s == 2 and w.prev == "v":
                    dve.wait_ge(misc_full, (w.misc_n + 1 + ONE).value())
                    nc.vector.tensor_copy(v_n[:, :, :].rearrange("p b d -> p (b d)"), misc[:, :]).then_inc(v_ready, 1)
                    dve.drain().then_inc(misc_free, 1)
                if s == 2 and at:
                    dve_denominator(dve, at, 0)
                if s == 2 and w.prev == "z":
                    dve.wait_ge(z_exp_ready, (w.prev_n + 1).value())
                    nc.vector.tensor_scalar(z_exp[:, :], z_exp[:, :], 1.0, None, ALU.add)
                    dve.drain()
                    nc.vector.reciprocal(z_exp[:, :T // 2], z_exp[:, :T // 2])
                if s == 3 and two:
                    dve_scores(dve, at, 1)
                if s == 4 and two:
                    dve_denominator(dve, at, 1)
                if s == 4 and w.prev == "z":
                    nc.vector.reciprocal(z_exp[:, T // 2:], z_exp[:, T // 2:])
                if s == 5 and w.prev == "z":
                    dve.drain()
                    nc.vector.tensor_tensor(z_t[:, :], z_t[:, :], z_exp[:, :], ALU.mult).then_inc(z_ready, 1)
                if s == 5 and w.biased is not None:
                    for slot in range(2):
                        n = (w.biased - 6).times(2) + slot
                        nc.vector.tensor_scalar(bias_a[:, slot, :], dist_a[:, :], slopes[:, n.pick()], None, ALU.mult)
                        nc.vector.tensor_copy(sink_col[:, slot:slot + 1], col("sinks", n))
                    dve.drain()
                    nc.vector.tensor_scalar(neg_sink[:, :], sink_col[:, :], -1.0, None, ALU.mult)
                if s == 6 and w.first != "gate":
                    m = w.misc_n + (w.prev == "v")
                    dve.wait_ge(misc_full, (m + 1 + ONE).value())
                    nc.vector.tensor_scalar(var[:, :], misc[:, :], 1.0 / (P if w.first == "qc" else HEAD), EPS,
                                            ALU.mult, ALU.add).then_inc(var_ready, 1)
                    dve.drain().then_inc(misc_free, 1)
                if s == 7 and w.first != "gate":
                    rstd_newton(dve, rs[:, :], T, w.rs_n)
                    dst, ready, gain = {"kb": (k_t, k_ready, "kg_b"), "ka": (k_t, k_ready, "kg_a"),
                                        "qb": (q_t, q_ready, "qg_b"), "qa": (q_t, q_ready, "qg_a"),
                                        "qc": (q_t, q_ready, "qg_c")}[w.first]
                    dve.wait_ge(plain_ready, (w.rs_n - 7).value())
                    nc.vector.scalar_tensor_tensor(dst[:, :], plain[:, :], col(gain), rs[:, :],
                                                   ALU.mult, ALU.mult).then_inc(ready, 1)
                    dve.drain().then_inc(plain_used, 1)
            if at:
                dve.drain()
                dve.wait_ge(pv_done, (at.done + ONE).value())
                nc.vector.tensor_tensor(tile(x3, at.tile), ctx_out[:, :], z_t[:, :], ALU.mult).then_inc(ctx_free, 1)

        def pool_window(pool, w):
            at = w.attention
            if at:
                for slot in range(at.heads):
                    head = at.head + slot
                    pool.wait_ge(rden_ready, (head + 1).value())
                    for n in range(NB):
                        seg = probs[:, slot, OFF[at.kind][n]:OFF[at.kind][n] + LEN[at.kind][n]]
                        by = rden[:, 4 * slot + n:4 * slot + n + 1].to_broadcast([P, LEN[at.kind][n]])
                        nc.gpsimd.tensor_tensor(seg, seg, by, ALU.mult).then_inc(probs_ready, 1)
            if w.loads is None:
                return
            kind, n = w.loads
            if kind == "b":
                pool.wait_ge(score_read, (n.times(8) + 1 + ONE).value())
                for slot in range(2):
                    row = n.times(2) + slot
                    pool.dma_start(neg_c[:, slot, :], c_store[row.pick(), :].to_broadcast([P, T])).then_inc(neg_c_loaded[slot], 16)
            else:
                pool.wait_ge(pv_done, (n + 24 + ONE).value())
                pool.dma_start(k_t[:, :MEM], mkv_store[n.pick(), :, :].rearrange("a p t -> p (a t)")).then_inc(k_loaded, 16)
                pool.dma_start(v_n[:, :2, :].rearrange("p b d -> p (b d)"),
                               mkv_store[(n + HEADS_C).pick(), :, :].rearrange("a p t -> p (a t)")).then_inc(v_loaded, 16)

        def windows(eng, run, extra=None):
            gb, rb, ga, ra, gc, rc = (FIRST["b"], RESULT["b"], FIRST["a"], RESULT["a"], FIRST["c"], RESULT["c"])

            def b_keys(j, attention):
                run(eng, Window(At(gb + 4 * j.c, 4 * j.k, j.i), At(rb + 4 * j.c, 4 * j.k, j.i),
                                "kb", "z" if attention else "f", j - 1, j.times(3) + 8, j.times(2) + 8,
                                attention=attention, extra=extra if attention is None else None))

            def b_queries(j, more=None):
                run(eng, Window(At(gb + 2 + 4 * j.c, 4 * j.k, j.i), At(rb + 2 + 4 * j.c, 4 * j.k, j.i),
                                "qb", "v", None, j.times(3) + 9, j.times(2) + 9, loads=("b", j), extra=more))

            b_keys(At(0), None)
            b_queries(At(0), (lambda s: extra(s + 8)) if extra else None)
            with steps(eng, 1, HEADS_B // 2) as i:
                j = At(0, 1, i)
                b_keys(j, Attention("b", j - 1, j))
                b_queries(j)
            for c in range(2):
                g, r, m = ga + 8 * c, ra + 8 * c, 26 + 5 * c
                last = Attention("b", At(5), At(6)) if c == 0 else Attention("a", At(8), At(7))
                run(eng, Window(At(g), At(r), "ka", "z", At(5 + 3 * c), At(m), At(20 + 4 * c), attention=last))
                run(eng, Window(At(g + 2), At(r + 2), "qa", "v", None, At(m + 1), At(21 + 4 * c), biased=At(6 + 3 * c)))
                with steps(eng, 1, GROUPS) as i:
                    job = At(6 + 3 * c, 1, i)
                    run(eng, Window(At(g + 2, 2, i), At(r + 2, 2, i), "qa", "z", job - 1, At(m + 2, 1, i),
                                    At(21 + 4 * c, 1, i), attention=Attention("a", job - 1, At(7 + c)), biased=job))
            run(eng, Window(At(gc), At(rc), "qc", "z", At(11), At(36), At(28), attention=Attention("a", At(11), At(8)),
                            loads=("c", At(0))))
            with steps(eng, 1, HEADS_C) as i:
                run(eng, Window(At(gc, 2, i), At(rc, 2, i), "qc", "z", At(11, 1, i), At(36, 1, i), At(28, 1, i),
                                attention=Attention("c", At(11, 1, i), At(0, 1, i)), loads=("c", At(0, 1, i))))
            run(eng, Window(At(FIRST["gated"]), At(RESULT["gated"]), "gate", "z", At(15), out_n=At(0),
                            attention=Attention("c", At(15), At(4))))

        def mem_beats(eng, run, *first):
            run(At(0), None, *first)
            for n in range(1, HEADS_C + 1):
                run(At(n), "k")
            for n in range(HEADS_C + 1, 2 * HEADS_C):
                run(At(n), "v")

        block = ctx.enter_context(nc.Block())

        @block.sync
        def _(sp):
            for name, dst in (("ident", ident), ("ones", ones), ("blocks", blocks), ("slopes", slopes)):
                a, b = CONST[name]
                sp.dma_start(dst[:, :], const_in[:, a:b]).then_inc(consts_loaded, 16)
            a, b = CONST["edges"]
            sp.dma_start(edges[:, :, :].rearrange("p a b -> p (a b)"), const_in[:, a:b]).then_inc(consts_loaded, 16)
            a, b = CONST["causal"]
            sp.dma_start(tmp[:, 1, :P], const_in[:, a:b]).then_inc(mask_loaded, 16)
            sp.dma_start(cols[:, :], cols_in).then_inc(cols_loaded, 16)
            for s in range(4):
                row = (s % 2 * KT + s // 2) * P
                sp.dma_start(wmod_sb[s][:, :], wmod[row:row + P, :]).then_inc(wmod_loaded[s], 16)
            load_panel(sp, At(0))
            with steps(sp, 1, 2 * HEADS_C) as i:
                load_panel(sp, At(0, 1, i))
                for s in range(4):
                    rows = wmod[At((s % 2 * KT + s // 2) * P, 2 * P, i).pick(P), :]
                    sp.wait_ge(wmod_used, At(s - 3, 4, i).value())
                    sp.dma_start(wmod_sb[s][:, :], rows).then_inc(wmod_loaded[s], 16)
            with steps(sp, FIRST["pool_in"], FIRST["pool_out"]) as i:
                load_panel(sp, At(0, 1, i))
            def end_loads(m, slot, again=True):
                gate_rows, x_rows = wmod[(m.times(P) + 2 * KT * P).pick(P), :], xT[m.times(P).pick(P), :]
                load_panel(sp, m + FIRST["pool_out"])
                if not again and slot == 0:
                    sp.wait_ge(w_used, 4 * FIRST["pool_out"])
                    sp.wait_ge(sums_zeroed, 2)
                if again:
                    sp.wait_ge(wmod_used, (m + (2 * KT - 1)).value())
                sp.dma_start(wmod_sb[slot][:, :], gate_rows).then_inc(wmod_loaded[slot], 16)
                if again:
                    sp.wait_ge(x1_ready, (m - 1).value())
                sp.dma_start(x_in[:, slot, :], x_rows).then_inc(x_in_loaded[slot], 16)
            for slot in range(2):
                end_loads(At(slot), slot, again=False)
            with steps(sp, 1, KT // 2) as i:
                for slot in range(2):
                    end_loads(At(slot, 2, i), slot)
            with steps(sp, FIRST["forget"], FIRST["out"]) as i:
                load_panel(sp, At(0, 1, i))
            def back_loads(n, slot, again=True):
                src = x_store[n.pick(), :, :].rearrange("a p t -> p (a t)")
                load_panel(sp, n + FIRST["out"])
                if again:
                    sp.wait_ge(result_ready, (n - 1).value())
                else:
                    sp.wait_ge(xp_stored[slot], 16 * KT // 2)
                    sp.wait_ge(y_ready, KT)
                sp.dma_start(x_back[:, slot, :], src).then_inc(
                    x_back_loaded[slot], 16)
            for slot in range(2):
                back_loads(At(slot), slot, again=False)
            with steps(sp, 1, KT // 2) as i:
                for slot in range(2):
                    back_loads(At(slot, 2, i), slot)

        @block.tensor
        def _(pe):
            pe.wait_ge(consts_loaded, 16 * 5)
            for which, width in ((0, MEM), (1, T)):
                for k in range(KT):
                    pe.wait_ge(square_ready, KT * which + k + 1)
                    nc.tensor.matmul(score[which][:, :width], ones[:, :], squares[:, k % 2, :width],
                                     start=k == 0, stop=k == KT - 1).then_inc(square_used, 1)

            def mem_panel(n, kind, ready=None):
                def later():
                    if kind == "k":
                        pe_squares(pe, msrc0, ones, MEM, n - 1)
                    if kind == "v":
                        pe_turn_values(pe, msrc0, MEM, n - 1)
                panel(pe, n, n, memn_hi, memn_lo, {2: later}, tokens=MEM, ready=ready)
            mem_beats(pe, mem_panel, memn_ready)
            pe_turn_values(pe, msrc0, MEM, At(2 * HEADS_C - 1))

            g, r = FIRST["pool_in"], RESULT["pool_in"]
            panel(pe, At(g), At(r), x1_hi, x1_lo, ready=h_ready)
            panel(pe, At(g + 1), At(r + 1), x1_hi, x1_lo)
            with steps(pe, 1, KT) as i:
                panel(pe, At(g, 2, i), At(r, 2, i), x1_hi, x1_lo)
                panel(pe, At(g + 1, 2, i), At(r + 1, 2, i), x1_hi, x1_lo)
            for grp in range(4):
                pe.wait_ge(pooled_ready, 4 * grp + 4)
                for q in range(4):
                    r = At(RESULT["group"] + 4 * grp + q)
                    pe.wait_ge(acc_free[r.parity()], (r.half() + ONE).value())
                    pe.wait_ge(lo_ready, 4 * (FIRST["group"] + grp) + q + 1)
                    for k in range(4):
                        mm = tile_products(acc[r.parity()], q, k, x2_hi, x2_lo, 4 * grp + k, k == 0, k == 3)
                    mm.then_inc(w_used, 1)
            g, r = FIRST["pool_out"], RESULT["pool_out"]
            panel(pe, At(g), At(r), x1_hi, x1_lo, ready=yg_ready)
            panel(pe, At(g + 1), At(r + 1), x1_hi, x1_lo)
            with steps(pe, 1, KT // 2) as i:
                for n in range(2):
                    panel(pe, At(g + n, 2, i), At(r + n, 2, i), x1_hi, x1_lo)
            pe.wait_ge(sq_added, 2 * KT + ONE)
            for which, total in ((0, sum_a), (1, sum_b)):
                nc.tensor.matmul(score[which][:, :], ones[:, :], total[:, :], start=True, stop=True).then_inc(sums_full, 1)
            panel(pe, At(FIRST["forget"]), At(RESULT["forget"]), x1_hi, x1_lo, ready=hn_ready)
            windows(pe, pe_window)

            def branches(g, r, ready=None):
                tiles = HEADS_A * HEAD // P, HEADS_B * HEAD // P, HEADS_C
                ends = [sum(tiles[:n + 1]) for n in range(3)]
                for q in range(4):
                    if ready is not None:
                        pe.wait_ge(ready, 4 * (q + 1))
                    pe.wait_ge(lo_ready, (g.times(4) + (q + 1)).value())
                    for k in range(4):
                        kk = 4 * q + k
                        b = sum(kk >= e for e in ends)
                        first = kk == 0 or kk in ends
                        if first:
                            pe.wait_ge(acc_free[(r + b).parity()], ((r + b).half() + ONE).value())
                        mm = tile_products(acc[(r + b).parity()], q, k, x2_hi, x2_lo, kk, first, kk + 1 in ends)
                    mm.then_inc(w_used, 1)
            g, r = FIRST["gated"], RESULT["gated"]
            panel(pe, At(g + 2), At(r + 2), x1_hi, x1_lo)
            branches(At(g + 3), At(r + 3), yz_ready)
            with steps(pe, 1, KT) as i:
                for b in range(3):
                    panel(pe, At(g + b, 4, i), At(r + b, 6, i), x1_hi, x1_lo)
                branches(At(g + 3, 4, i), At(r + 3, 6, i))
            g, r = FIRST["out"], RESULT["out"]
            panel(pe, At(g), At(r), x1_hi, x1_lo, ready=y_split)
            panel(pe, At(g + 1), At(r + 1), x1_hi, x1_lo)
            with steps(pe, 1, KT // 2) as i:
                for n in range(2):
                    panel(pe, At(g + n, 2, i), At(r + n, 2, i), x1_hi, x1_lo)

        @block.scalar
        def _(act):
            act.dma_start(mem_raw[:, :, :], memT.rearrange("(k p) t -> p k t", p=P)).then_inc(mem_loaded, 16)
            act.dma_start(x3[:, :, :], xT.rearrange("(k p) t -> p k t", p=P)).then_inc(x_loaded, 16)
            act.dma_start(c_rows[:, :], cvec.to_broadcast([P, D])).then_inc(c_loaded, 16)
            act.wait_ge(mem_loaded, 16)
            for k in range(KT):
                if At(k - 1).positive():
                    act.wait_ge(square_used, At(k - 1).value())
                nc.scalar.activation(squares[:, k % 2, :MEM], mem_raw[:, k, :], ACT.Square).then_inc(square_ready, 1)
            act.wait_ge(x_loaded, 16)
            for k in range(KT):
                if At(KT + k - 1).positive():
                    act.wait_ge(square_used, At(KT + k - 1).value())
                nc.scalar.activation(squares[:, k % 2, :], x3[:, k, :], ACT.Square).then_inc(square_ready, 1)
            act.wait_ge(c_loaded, 16)
            nc.scalar.activation(c_rows[:, :], c_rows[:, :], ACT.Silu).then_inc(c_ready, 1)
            rstd_guess(act, MEM, At(0))
            rstd_guess(act, T, At(1))
            for q in range(3):
                split_hi(act, At(q - 3))


            def mem_source(n, kind):
                act.wait_ge(w_used, (n.times(4)).value())
                act.wait_ge(misc_full, (n - 1 + ONE).value())
                before = acc[(n - 1).parity()][:, :MEM]
                nc.scalar.activation(msrc0[:, :], before, ACT.Square if kind == "k" else ACT.Copy).then_inc(msrc_ready, 1)
                if kind == "v":
                    act.drain().then_inc(acc_free[(n - 1).parity()], 1)

            def mem_beat(n, kind):
                for s in range(4):
                    split_hi(act, n.times(4) + s)
                    if s == 0 and kind:
                        mem_source(n, kind)
                    if s == 2 and kind == "k":
                        rstd_guess(act, MEM, n + 1)
            mem_beats(act, mem_beat)
            mem_source(At(2 * HEADS_C), "v")

            def sigmoid_of_g(n):
                r = n.times(2) + (RESULT["pool_in"] + 1)
                act.wait_ge(w_used, ((n.times(2) + (FIRST["pool_in"] + 2)).times(4)).value())
                act.wait_ge(sig_used, (n + ONE).value())
                nc.scalar.activation(sig0[:, :], acc[r.parity()][:, :], ACT.Sigmoid).then_inc(sig_ready, 1)

            def pool_in_beats(n, peeled=False):
                t = (n.times(2) + FIRST["pool_in"]).times(4)
                r = n.times(2) + RESULT["pool_in"]
                for s in range(8):
                    split_hi(act, t + s)
                    if s == 0 and not peeled:
                        sigmoid_of_g(n - 1)
                    if s == 4:
                        act.wait_ge(w_used, (t + 4).value())
                        if n.positive():
                            act.wait_ge(urow_used, n.value())
                        nc.scalar.activation(urow[:, PAD:PAD + T], acc[r.parity()][:, :], ACT.Copy).then_inc(urow_ready, 1)
                        act.drain().then_inc(acc_free[r.parity()], 1)
            act.wait_ge(urow_zeroed, 1)
            pool_in_beats(At(0), peeled=True)
            with steps(act, 1, KT) as i:
                pool_in_beats(At(0, 1, i))
            for n in range(KT):
                split_hi(act, At(4 * FIRST["group"] + n))
                if n == 0:
                    sigmoid_of_g(At(KT - 1))

            def squares_of_x1(m):
                act.wait_ge(x1_ready, (m + 1).value())
                act.wait_ge(sq_added, (m.times(2) + ONE).value())
                nc.scalar.activation(sq_a[:, :], tile(x3, m), ACT.Square).then_inc(sq_ready, 1)
                nc.scalar.activation(sq_b[:, :], tile(x3, m), ACT.Square, scale=col("final_g", m)).then_inc(sq_ready, 1)

            def pool_out_beat(m, peeled=False):
                t = (m + FIRST["pool_out"]).times(4)
                for s in range(4):
                    split_hi(act, t + s)
                    if peeled and s == 0:
                        act.wait_ge(w_used, t.value())
                        act.dma_start(c_rows3[:, :], cvec.to_broadcast([P, D])).then_inc(gate_c_loaded, 16)
                    if peeled and s == 2:
                        act.wait_ge(gate_c_loaded, 16)
                        nc.scalar.activation(c_rows3[:, :], c_rows3[:, :], ACT.Silu).then_inc(c_ready, 1)
                    if not peeled and s == 1:
                        squares_of_x1(m - 1)
            pool_out_beat(At(0), peeled=True)
            pool_out_beat(At(1))
            with steps(act, 1, KT // 2) as i:
                for slot in range(2):
                    pool_out_beat(At(slot, 2, i))
            squares_of_x1(At(KT - 1))
            rstd_guess(act, T, At(6))
            rstd_guess(act, T, At(7))
            act.wait_ge(wmod_used, 3 * KT)
            act.dma_start(dist_a[:, :], dist_in).then_inc(dist_loaded, 16)
            for s in range(4):
                split_hi(act, At(4 * FIRST["forget"] + s))
            act.drain().then_inc(turned_copied, 1)
            windows(act, act_window)

            g, r = FIRST["gated"], RESULT["gated"]

            def gated_beat(n, b):
                t = (n.times(4) + (g + b)).times(4)
                for s in range(4):
                    split_hi(act, t + s)
                    if s == 0 and b > 0:
                        act_gate(act, n.times(6) + (r + b - 1), t, b - 1, n)
            for b in (2, 3):
                gated_beat(At(0), b)
            with steps(act, 1, KT) as i:
                for b in range(4):
                    gated_beat(At(0, 1, i), b)

            def store_result(n):
                act.wait_ge(result_ready, (n + 1).value())
                act.dma_start(out[n.times(P).pick(P), :], result[:, n.parity(), :]).then_inc(result_stored[n.parity()], 16)

            def out_beat(n, peeled=False):
                for s in range(4):
                    split_hi(act, (n + FIRST["out"]).times(4) + s)
                    if s == 1 and not peeled:
                        store_result(n - 1)
            out_beat(At(0), peeled=True)
            out_beat(At(1))
            with steps(act, 1, KT // 2 - 1) as i:
                for slot in range(2):
                    out_beat(At(slot, 2, i))
            out_beat(At(KT - 2))
            out_beat(At(KT - 1))
            store_result(At(KT - 1))
            for n in range(2):
                act.wait_ge(result_stored[n], 16 * KT // 2 + ONE)

        @block.vector
        def _(dve):
            for one in from_one:
                dve.drain().then_inc(one, 1)
            dve.wait_ge(consts_loaded, 16 * 5)
            dve.wait_ge(mask_loaded, 16)
            dve.wait_ge(cols_loaded, 16)
            nc.vector.tensor_copy(ident_b[:, :], ident[:, :])
            nc.vector.tensor_copy(causal_b[:, :], tmp[:, 1, :P])
            nc.vector.tensor_tensor(hn_g[:, :], col("final_g"), col("norm_g"), ALU.mult)
            for name, width in (("qg_a", HEAD), ("qg_b", HEAD), ("qg_c", P)):
                nc.vector.tensor_scalar(col(name), col(name), width ** -0.5, None, ALU.mult)
            dve.drain()

            def variance(source, width, features):
                nc.vector.tensor_scalar(var[:, :width], source, 1.0 / features, EPS, ALU.mult, ALU.add).then_inc(var_ready, 1)

            r_mem, r_x = mem_out, tmp[:, 1, :]
            dve.wait_ge(square_used, KT)
            variance(score[0][:, :MEM], MEM, D)
            rstd_newton(dve, r_mem[:, :], MEM, At(0))
            dve.wait_ge(square_used, 2 * KT)
            variance(score[1][:, :], T, D)
            rstd_newton(dve, r_x, T, At(1))
            dve.drain().then_inc(rx_ready, 1)
            for q in range(3):
                split_lo(dve, At(q - 3))
            with steps(dve, 0, KT) as i:
                k = At(0, 1, i)
                nc.vector.scalar_tensor_tensor(tmp[:, 0, :MEM], tile(mem_raw, k), col("mem_g", k), r_mem[:, :],
                                               ALU.mult, ALU.mult)
                split_act(dve, tmp[:, 0, :MEM], tile(memn_hi, k), tile(memn_lo, k), memn_ready)
            dve.wait_ge(c_ready, 1)

            def mod_rows(s, count):
                dve.wait_ge(wmod_loaded[s], count.value())
                nc.vector.memset(arrived[:, s:s + 1], 0.0)
                nc.vector.tensor_tensor_reduce(out=wmod_sb[s][:, :], in0=wmod_sb[s][:, :],
                                               in1=c_rows[:, :], scale=1.0, scalar=0.0,
                                               op0=ALU.mult, op1=ALU.add, accum_out=mod_part[:, s:s + 1]).then_inc(wmod_used, 1)
                dve.drain()

            def mem_finish(n, kind, s):
                if s == 2:
                    dve.wait_ge(misc_full, (n + ONE).value())
                    if kind == "k":
                        variance(misc[:, :MEM], MEM, P)
                    else:
                        if (n - 1).times(16).positive():
                            dve.wait_ge(mem_out_stored, (n - 1).times(16).value())
                        nc.vector.tensor_copy(mem_out[:, :], misc[:, :MEM]).then_inc(mem_out_ready, 1)
                    dve.drain().then_inc(misc_free, 1)
                if s == 3 and kind == "k":
                    rstd_newton(dve, rs[:, :MEM], MEM, n + 1)
                    if (n - 1).times(16).positive():
                        dve.wait_ge(mem_out_stored, (n - 1).times(16).value())
                    before = (n - 1).parity()
                    nc.vector.scalar_tensor_tensor(mem_out[:, :], acc[before][:, :MEM], col("kg_c"), rs[:, :MEM],
                                                   ALU.mult, ALU.mult).then_inc(mem_out_ready, 1)
                    dve.drain().then_inc(acc_free[before], 1)

            def mem_beat(n, kind):
                for s in range(4):
                    split_lo(dve, n.times(4) + s)
                    if kind:
                        mem_finish(n, kind, s)
                    mod_rows(s, (n + 1).times(16))
                    k = n.times(2) + s // 2
                    if s % 2 == 0:
                        nc.vector.tensor_tensor(mod[:, k.pick()], mod_part[:, s:s + 1], col("b_mod", k), ALU.add)
                    else:
                        nc.vector.scalar_tensor_tensor(mod[:, (k + KT).pick()], mod_part[:, s:s + 1], 1.0,
                                                       col("b_mod", k + KT), ALU.add, ALU.add)
                        dve.drain()
                        dve.wait_ge(xr_ready, (k + 1).value())
                        nc.vector.tensor_scalar(tmp[:, 0, :], tile(x3, k), mod[:, (k + KT).pick()], mod[:, k.pick()],
                                                ALU.mult, ALU.add)
                        split_act(dve, tmp[:, 0, :], tile(x1_hi, k), tile(x1_lo, k), h_ready)
            mem_beats(dve, mem_beat)
            mem_finish(At(2 * HEADS_C), "v", 2)

            dve.wait_ge(mem_out_stored, 16 * 2 * HEADS_C)
            nc.vector.memset(urow[:, :PAD], 0.0)
            nc.vector.memset(urow[:, PAD + T:], 0.0)
            dve.drain().then_inc(urow_zeroed, 1)

            def silu_of_g(n):
                r = n.times(2) + (RESULT["pool_in"] + 1)
                dve.wait_ge(sig_ready, (n + 1).value())
                nc.vector.tensor_tensor(tile(x3, n), acc[r.parity()][:, :], sig0[:, :], ALU.mult).then_inc(sig_used, 1)
                dve.drain().then_inc(acc_free[r.parity()], 1)

            def ends(row, at):
                return row[:, at:at + T].rearrange("p (a b) -> p a b", b=PAD)[:, 0:T // PAD:T // PAD - 1, :]

            def pool_in_beats(n, grp, peeled=False):
                window = POOL_WINDOWS[grp]
                t = (n.times(2) + FIRST["pool_in"]).times(4)
                level = window.bit_length() - 1
                total = wsum[(level - 1) % 2]
                at = PAD - window // 2
                for s in range(8):
                    split_lo(dve, t + s)
                    if s == 1 and not peeled:
                        silu_of_g(n - 1)
                    if s == 5:
                        dve.wait_ge(urow_ready, (n + 1).value())
                        source = urow
                        for j in range(level):
                            width = ROW - (1 << (j + 1)) + 1
                            nc.vector.tensor_tensor(wsum[j % 2][:, :width], source[:, :width],
                                                    source[:, 1 << j:(1 << j) + width], ALU.add)
                            dve.drain()
                            source = wsum[j % 2]
                    if s == 6:
                        nc.vector.scalar_tensor_tensor(tmp[:, 0, :], total[:, at:at + T], 1.0 / window,
                                                       urow[:, PAD:PAD + T], ALU.mult, ALU.subtract)
                        dve.drain()
                        table = edges[:, grp, :].rearrange("p (a b) -> p a b", b=PAD)
                        nc.vector.tensor_tensor(ends(tmp[:, 0, :], 0), ends(total, at), table, ALU.mult)
                        dve.drain()
                        nc.vector.tensor_tensor(ends(tmp[:, 0, :], 0), ends(tmp[:, 0, :], 0), ends(urow, PAD),
                                                ALU.subtract).then_inc(urow_used, 1)
                    if s == 7:
                        split_act(dve, tmp[:, 0, :], tile(x2_hi, n), tile(x2_lo, n), pooled_ready)
            for grp in range(4):
                if grp == 0:
                    pool_in_beats(At(0), 0, peeled=True)
                with steps(dve, max(4 * grp, 1), 4 * grp + 4) as i:
                    pool_in_beats(At(0, 1, i), grp)

            def grouped(n):
                r = At(RESULT["group"] + n)
                dve.wait_ge(w_used, 4 * FIRST["group"] + n + 1)
                nc.vector.scalar_tensor_tensor(tmp[:, 0, :], acc[r.parity()][:, :], col("pool_scale", n), x3[:, n, :],
                                               ALU.mult, ALU.mult)
                dve.drain().then_inc(acc_free[r.parity()], 1)
                split_act(dve, tmp[:, 0, :], x1_hi[:, n, :], x1_lo[:, n, :], yg_ready)
            for n in range(KT):
                split_lo(dve, At(4 * FIRST["group"] + n))
                if n == 0:
                    silu_of_g(At(KT - 1))
                else:
                    grouped(n - 1)

            def residual(m):
                r = m + RESULT["pool_out"]
                dve.wait_ge(w_used, (m + FIRST["pool_out"] + 1).times(4).value())
                dve.wait_ge(x_in_loaded[m.parity()], ((m.half() + 1).times(16)).value())
                nc.vector.scalar_tensor_tensor(tile(x3, m), acc[r.parity()][:, :], mod[:, (m + 2 * KT).pick()],
                                               x_in[:, m.parity(), :], ALU.mult, ALU.add).then_inc(x1_ready, 1)
                dve.drain().then_inc(acc_free[r.parity()], 1)

            def pool_out_beat(m, peeled=False):
                for s in range(4):
                    split_lo(dve, (m + FIRST["pool_out"]).times(4) + s)
                    if s == 0:
                        if peeled:
                            grouped(KT - 1)
                        else:
                            residual(m - 1)
                    if s == 2:
                        slot = m.parity()
                        if peeled:
                            dve.wait_ge(c_ready, 2)
                        dve.wait_ge(wmod_loaded[slot], ((m.half() + (KT // 2 + 1)).times(16)).value())
                        nc.vector.memset(arrived[:, slot:slot + 1], 0.0)
                        nc.vector.tensor_tensor_reduce(
                            out=wmod_sb[slot][:, :], in0=wmod_sb[slot][:, :], in1=c_rows3[:, :], scale=1.0, scalar=0.0,
                            op0=ALU.mult, op1=ALU.add, accum_out=mod_part[:, slot:slot + 1]).then_inc(wmod_used, 1)
                        dve.drain()
                        k = m + 2 * KT
                        nc.vector.tensor_tensor(mod[:, k.pick()], mod_part[:, slot:slot + 1], col("b_mod", k), ALU.add)
                        dve.drain()
            pool_out_beat(At(0), peeled=True)
            pool_out_beat(At(1))
            with steps(dve, 1, KT // 2) as i:
                for slot in range(2):
                    pool_out_beat(At(slot, 2, i))
            residual(At(KT - 1))

            dve.wait_ge(sums_full, 1)
            variance(score[0][:, :], T, D)
            rstd_newton(dve, r_one[:, :], T, At(6))
            dve.wait_ge(sums_full, 2)
            nc.vector.scalar_tensor_tensor(var[:, :], score[1][:, :], 1.0 / D, r_one[:, :], ALU.mult, ALU.mult)
            dve.drain().then_inc(score_read, 1)
            nc.vector.tensor_tensor(var[:, :], var[:, :], r_one[:, :], ALU.mult)
            dve.drain()
            nc.vector.tensor_scalar(var[:, :], var[:, :], EPS, None, ALU.add).then_inc(var_ready, 1)
            rstd_newton(dve, rs[:, :], T, At(7))
            nc.vector.tensor_tensor(r_both[:, :], rs[:, :], r_one[:, :], ALU.mult)
            nc.vector.memset(zero_c[:, :], 0.0)
            dve.drain()
            for s in range(4):
                with steps(dve, 4 * s, 4 * s + 4) as i:
                    k = At(0, 1, i)
                    nc.vector.scalar_tensor_tensor(tmp[:, 0, :], tile(x3, k), hn_g[:, k.pick()], r_both[:, :],
                                                   ALU.mult, ALU.mult)
                    split_act(dve, tmp[:, 0, :], tile(x1_hi, k), tile(x1_lo, k), hn_ready)
                split_lo(dve, At(4 * FIRST["forget"] + s))
            dve.drain()
            dve.wait_ge(dist_loaded, 16)

            def x_prime(k):
                dve.wait_ge(xp_stored[k % 2], 16 * (k // 2))
                nc.vector.scalar_tensor_tensor(tmp[:, k % 2, :], x3[:, k, :], col("final_g", k), r_one[:, :],
                                               ALU.mult, ALU.mult).then_inc(xp_ready, 1)
            windows(dve, dve_window, x_prime)

            g, r = FIRST["gated"], RESULT["gated"]

            def branch(n, b):
                t = (n.times(4) + (g + 3)).times(4)
                dve.wait_ge(w_used, (t + (b + 2)).value())
                dve.wait_ge(gsig_ready, (n.times(3) + (b + 1)).value())
                bank_n = (n.times(6) + (r + 3 + b)).parity()
                nc.vector.tensor_tensor(part[:, min(b, 1), :], acc[bank_n][:, :], gate_sig[:, b, :], ALU.mult)
                dve.drain().then_inc(acc_free[bank_n], 1)
                if b == 1:
                    nc.vector.tensor_tensor(part[:, 0, :], part[:, 0, :], part[:, 1, :], ALU.add)
                    dve.drain()
                if b == 2:
                    nc.vector.tensor_tensor(tile(x3, n), part[:, 0, :], part[:, 1, :], ALU.add).then_inc(y_ready, 1)

            def gated_beat(n, b, peeled=False):
                t = (n.times(4) + (g + b)).times(4)
                for s in range(4):
                    split_lo(dve, t + s)
                    if s == 0 and b == 0:
                        branch(n - 1, 2)
                    if peeled and b == 2:
                        dve.drain()
                        with steps(dve, 4 * s, 4 * s + 4) as i:
                            k = At(0, 1, i)
                            split_act(dve, tile(x3, k), tile(x2_hi, k), tile(x2_lo, k), yz_ready)
                    if b == 3 and s >= 2:
                        branch(n, s - 2)
            for b in (2, 3):
                gated_beat(At(0), b, peeled=True)
            with steps(dve, 1, KT) as i:
                for b in range(4):
                    gated_beat(At(0, 1, i), b)
            branch(At(KT - 1), 2)

            def finish(n):
                rr = n + RESULT["out"]
                dve.wait_ge(w_used, (n + FIRST["out"] + 1).times(4).value())
                dve.wait_ge(x_back_loaded[n.parity()], ((n.half() + 1).times(16)).value())
                dve.wait_ge(result_stored[n.parity()], (n.half().times(16) + ONE).value())
                nc.vector.tensor_tensor(result[:, n.parity(), :], acc[rr.parity()][:, :], x_back[:, n.parity(), :],
                                        ALU.add).then_inc(result_ready, 1)
                dve.drain().then_inc(acc_free[rr.parity()], 1)

            def out_beat(n, peeled=False):
                for s in range(4):
                    if peeled:
                        with steps(dve, 4 * s, 4 * s + 4) as i:
                            k = At(0, 1, i)
                            split_act(dve, tile(x3, k), tile(x1_hi, k), tile(x1_lo, k), y_split)
                    split_lo(dve, (n + FIRST["out"]).times(4) + s)
                    if s == 0 and not peeled:
                        finish(n - 1)
            out_beat(At(0), peeled=True)
            out_beat(At(1))
            with steps(dve, 1, KT // 2 - 1) as i:
                for slot in range(2):
                    out_beat(At(slot, 2, i))
            out_beat(At(KT - 2))
            out_beat(At(KT - 1))
            finish(At(KT - 1))

        @block.gpsimd
        def _(pool):
            pool.wait_ge(rx_ready, 1)
            with steps(pool, 0, KT) as i:
                row = tile(x3, At(0, 1, i))
                nc.gpsimd.tensor_tensor(row, row, tmp[:, 1, :], ALU.mult).then_inc(xr_ready, 1)
            with steps(pool, 0, 2 * HEADS_C) as i:
                n = At(0, 1, i)
                pool.wait_ge(mem_out_ready, (n + 1).value())
                pool.dma_start(mkv_store[n.pick(), :, :].rearrange("a p t -> p (a t)"), mem_out[:, :]).then_inc(mem_out_stored, 16)
            pool.wait_ge(sig_used, KT + ONE)
            for total in (sum_a, sum_b):
                nc.gpsimd.memset(total[:, :], 0.0).then_inc(sums_zeroed, 1)
            pool.wait_ge(sums_zeroed, 2)
            with steps(pool, 0, KT) as i:
                for which, (total, square) in enumerate(((sum_a, sq_a), (sum_b, sq_b))):
                    pool.wait_ge(sq_ready, At(which + 1, 2, i).value())
                    pool.wait_ge(sq_added, (At(which, 2, i) + ONE).value())
                    nc.gpsimd.tensor_tensor(total[:, :], total[:, :], square[:, :], ALU.add).then_inc(sq_added, 1)
            with steps(pool, 0, KT // 2) as i:
                for slot in range(2):
                    k = At(slot, 2, i)
                    pool.wait_ge(xp_ready, (k + 1).value())
                    pool.dma_start(x_store[k.pick(), :, :].rearrange("a p t -> p (a t)"), tmp[:, slot, :]).then_inc(xp_stored[slot], 16)
            pool.wait_ge(c_neg_ready, 1)
            pool.dma_start(c_store, f_a[:HEADS_B, :]).then_inc(c_stored, 16)
            pool.wait_ge(c_stored, 16)
            windows(pool, pool_window)


def panels(w):
    k, n = w.shape
    return w.reshape(k // P, P, n // P, P).transpose(2, 1, 0, 3).reshape(n // P, P, k)


def weight_stream(inputs):
    w_in = inputs["w_in_2"][0]
    sizes = [HEADS_A * HEAD, HEADS_A * HEAD // GROUPS, HEADS_A * HEAD // GROUPS, HEADS_A * HEAD] + \
        [HEADS_B * HEAD] * 4 + [HEADS_B, HEADS_C * P, HEADS_C * P, 3 * D]
    qa, ka, va, za, qb, kb, vb, zb, fb, qc, zc, gates = np.split(w_in, np.cumsum(sizes)[:-1], axis=1)
    order = np.concatenate([np.arange(HEAD * h, HEAD * h + HEAD) for h in a_heads()])
    qa, za = panels(qa[:, order]), panels(za[:, order])
    ka, va = panels(ka), panels(va)
    qb, kb, vb, zb, qc, zc = (panels(w) for w in (qb, kb, vb, zb, qc, zc))
    mem = panels(inputs["w_mem_kv_2"][0])
    pool_in = panels(inputs["pool_w_in"][0])
    grouped = []
    for w in inputs["pool_w_grp"][0]:
        grouped.append(panels(w).transpose(1, 0, 2).reshape(1, P, 4 * w.shape[0]))
    forget = np.zeros((D, P), np.float32)
    forget[:, :HEADS_B] = fb
    gates = [panels(g) for g in np.split(gates, 3, axis=1)]
    branch = panels(np.concatenate([inputs["w_branch_a_2"][0][order], inputs["w_branch_b_2"][0],
                                    inputs["w_branch_c_2"][0]]))
    pool_out, w_out = panels(inputs["pool_w_out"][0]), panels(inputs["w_out_2"][0])

    def mixed(*parts):
        return np.stack(parts, axis=1).reshape(-1, P, D)
    a = []
    for c in range(2):
        a += [ka[c:c + 1], va[c:c + 1]]
        for g in range(GROUPS):
            j = GROUPS * c + g
            a += [qa[j:j + 1], za[j:j + 1]]
    return np.ascontiguousarray(np.concatenate(
        [mem, mixed(pool_in[:KT], pool_in[KT:]), *grouped, pool_out, panels(forget), mixed(kb, vb, qb, zb), *a,
         mixed(qc, zc), mixed(*gates, branch), w_out]))


def small_columns(inputs):
    def tiles(v):
        return v.reshape(-1, P).T
    forget = np.zeros((P, 1), np.float32)
    forget[:HEADS_B, 0] = inputs["b_forget_2"][0]

    def twice(name):
        return np.tile(inputs[name][0], 2).reshape(P, 1)
    sinks = np.broadcast_to(inputs["sinks_a_2"][0][a_heads()], (P, HEADS_A))
    return np.ascontiguousarray(np.concatenate(
        [tiles(inputs["b_mod"][0]), tiles(inputs["pool_scale"][0]), tiles(inputs["final_norm_g"]),
         tiles(inputs["norm_gain_2"][0]), tiles(inputs["mem_norm_gain_2"][0]), forget,
         twice("q_gain_a_2"), twice("k_gain_a_2"), twice("q_gain_b_2"), twice("k_gain_b_2"),
         inputs["q_gain_c_2"][0].reshape(P, 1), inputs["k_gain_c_2"][0].reshape(P, 1), sinks], axis=1))


def shape_constants():
    edge = np.zeros((4, 2 * PAD), np.float32)
    for j, w in enumerate(POOL_WINDOWS):
        for e, t in enumerate([*range(PAD), *range(T - PAD, T)]):
            edge[j, e] = 1.0 / (min(t + w // 2, T) - max(t - w // 2, 0))
    p = np.arange(P)
    slopes = 2.0 ** (-8.0 * (np.array(a_heads()) + 1) / HEADS_A)
    full = np.concatenate(
        [np.eye(P), np.ones((P, P)), (p[:, None] // HEAD == p[None, :] // HEAD).astype(float),
         np.where(p[None, :] > p[:, None], NEG, 0.0), np.broadcast_to(edge.reshape(1, -1), (P, edge.size)),
         np.broadcast_to(slopes, (P, HEADS_A))], axis=1).astype(np.float32)
    back = p[:, None] + P - np.arange(2 * P)[None, :]
    dist = np.where((back >= 0) & (back < P), -back, FAR).astype(np.float32)
    return full, dist


def kernel(**inputs):
    import concourse.bacc as bacc
    from concourse.bass_utils import run_bass_kernel_spmd

    inputs = {name: np.asarray(value) for name, value in inputs.items()}
    full, dist = shape_constants()
    arrays = {
        "stream": weight_stream(inputs),
        "w_mod_rows": np.ascontiguousarray(inputs["w_mod"][0].T),
        "c_row": np.ascontiguousarray(inputs["c"]),
        "x_features": np.ascontiguousarray(inputs["x"][0].T),
        "mem_features": np.ascontiguousarray(inputs["mem_2"][0].T),
        "columns": small_columns(inputs),
        "constants": full,
        "distances": dist,
    }
    nc = bacc.Bacc("TRN2", target_bir_lowering=False, num_devices=1)
    aps = [nc.dram_tensor(name, a.shape, F32, kind="ExternalInput").ap() for name, a in arrays.items()]
    stores = [nc.dram_tensor(name, shape, F32, kind="Internal").ap() for name, shape in
              (("x_store", (KT, P, T)), ("c_store", (HEADS_B, T)), ("mkv_store", (2 * HEADS_C, P, MEM)))]
    result = nc.dram_tensor("result_features", (D, T), F32, kind="ExternalOutput").ap()
    program(nc, *aps, *stores, result)
    got = run_bass_kernel_spmd(nc, [arrays], core_ids=[0])
    return np.ascontiguousarray(got.results[0]["result_features"].T).reshape(1, T, D)
```

```python
from contextlib import ExitStack, contextmanager

import numpy as np
import concourse.bass as bass
from concourse import mybir

F32 = mybir.dt.float32
F32R = mybir.dt.float32r
BF16 = mybir.dt.bfloat16
ACT = mybir.ActivationFunctionType
ALU = mybir.AluOpType

P = 128
D = 2048
T = 512
KT = D // P
NB = T // P
MEM = 256
POOL_WINDOWS = (2, 4, 8, 16)
PAD = POOL_WINDOWS[-1] // 2
ROW = T + 2 * PAD
HEAD = 64
GROUPS = 3
HEADS_A, HEADS_B, HEADS_C = 12, 12, 4
EPS = 1e-6
NEG = -1e30
FAR = -1e36

STAGES = [("pool_in", 2 * KT), ("group", 4), ("pool_out", KT), ("mem", 2 * HEADS_C), ("forget", 1),
          ("b", 4 * HEADS_B // 2), ("a", 2 * (2 + 2 * GROUPS)), ("c", 2 * HEADS_C),
          ("gated", 4 * KT), ("out", KT)]
FIRST = {}
_n = 0
for _name, _count in STAGES:
    FIRST[_name] = _n
    _n += _count
PANELS = _n
FRONT = 8
RESULT = {"pool_in": 2 - FRONT, "group": 26, "pool_out": 42, "mem": 58, "forget": 66, "b": 67, "a": 91, "c": 107,
          "gated": 115, "out": 211}

COLS = {}
_n = 0
for _name, _count in [("b_mod", 3 * KT), ("pool_scale", KT), ("final_g", KT), ("norm_g", KT), ("mem_g", KT),
                      ("b_forget", 1), ("qg_a", 1), ("kg_a", 1), ("qg_b", 1), ("kg_b", 1), ("qg_c", 1),
                      ("kg_c", 1), ("sinks", HEADS_A)]:
    COLS[_name] = (_n, _n + _count)
    _n += _count
NCOLS = _n
CONST = {}
_n = 0
for _name, _count in [("ident", P), ("ones", P), ("blocks", P), ("causal", P), ("edges", 4 * 2 * PAD),
                      ("slopes", HEADS_A)]:
    CONST[_name] = (_n, _n + _count)
    _n += _count
NCONST = _n


def a_heads():
    return [GROUPS * (2 * c + hh) + g for c in range(2) for g in range(GROUPS) for hh in range(2)]


class Step:

    def __init__(self, register, first):
        self.register, self.first = register, first


@contextmanager
def steps(eng, first, end):
    with eng.Fori(first, end) as register:
        yield Step(register, first)


class At:

    def __init__(self, c, k=0, i=None):
        self.c, self.k, self.i = c, k, i

    def __add__(self, n):
        return At(self.c + n, self.k, self.i)

    def __sub__(self, n):
        return At(self.c - n, self.k, self.i)

    def times(self, m):
        return At(self.c * m, self.k * m, self.i)

    def half(self):
        assert self.k % 2 == 0
        return At(self.c // 2, self.k // 2, self.i)

    def parity(self):
        assert self.k % 2 == 0
        return self.c % 2

    def value(self):
        return self.c if self.i is None else self.i.register * self.k + self.c

    def lowest(self):
        return self.c if self.i is None else self.i.first * self.k + self.c

    def positive(self):
        assert self.i is None or self.lowest() > 0
        return self.lowest() > 0

    def pick(self, size=1):
        return slice(self.c, self.c + size) if self.i is None else bass.ds(self.value(), size)


ONE = 1


def program(nc, stream, wmod, cvec, xT, memT, cols_in, const_in, dist_in, x_store, c_store, mkv_store, out):
    ctx = ExitStack()
    with ctx:
        def sem(name):
            return ctx.enter_context(nc.semaphore(name))

        KB = 1024
        top = [16512]

        def region(size):
            at = top[0]
            top[0] += size
            assert top[0] <= 229344, top[0]
            return at

        def sb(name, shape, dt, at):
            return nc.alloc_sbuf_tensor_at(name, shape, dt, offset=at)

        at_w = region(24 * KB)
        at_x1, at_x2, at_x3 = region(64 * KB), region(64 * KB), region(32 * KB)
        at_const = region(3712)
        at_scratch = region(20 * KB)

        w_raw = sb("w_raw", [P, 2, 8 * P], F32, at_w)
        w_hi = sb("w_hi", [P, 4, 4 * P], F32R, at_w + 8 * KB)
        w_lo = sb("w_lo", [P, 4, 4 * P], F32R, at_w + 16 * KB)
        x1_hi = sb("x1_hi", [P, KT, T], F32R, at_x1)
        x1_lo = sb("x1_lo", [P, KT, T], F32R, at_x1 + 32 * KB)
        x2_hi = sb("x2_hi", [P, KT, T], F32R, at_x2)
        x2_lo = sb("x2_lo", [P, KT, T], F32R, at_x2 + 32 * KB)
        x3 = sb("x3", [P, KT, T], F32, at_x3)

        cat = [at_const]

        def keep(name, shape, dt, size):
            at = cat[0]
            cat[0] += (size + 31) // 32 * 32
            assert cat[0] <= at_scratch
            return sb(name, shape, dt, at)

        ident = keep("ident", [P, P], F32, 512)
        ones = keep("ones", [P, P], F32, 512)
        blocks = keep("blocks", [P, P], F32, 512)
        edges = keep("edges", [P, 4, 2 * PAD], F32, 256)
        slopes = keep("slopes", [P, HEADS_A], F32, 48)
        ident_b = keep("ident_b", [P, P], BF16, 256)
        causal_b = keep("causal_b", [P, P], BF16, 256)
        cols = keep("cols", [P, NCOLS], F32, 4 * NCOLS)
        mod = keep("mod", [P, 3 * KT], F32, 4 * 3 * KT)
        hn_g = keep("hn_g", [P, KT], F32, 4 * KT)
        mod_part = keep("mod_part", [P, 4], F32, 16)
        neg_max = keep("neg_max", [P, 8], F32, 32)
        den = keep("den", [P, 8], F32, 32)
        rden = keep("rden", [P, 8], F32, 32)
        sink_exp = keep("sink_exp", [P, 8], F32, 32)
        sink_col = keep("sink_col", [P, 2], F32, 8)
        neg_sink = keep("neg_sink", [P, 2], F32, 8)
        arrived = keep("arrived", [P, 8], F32, 32)

        def col(name, n=None):
            a, b = COLS[name]
            if n is None:
                return cols[:, a:b]
            return cols[:, (n + a).pick()] if isinstance(n, At) else cols[:, a + n:a + n + 1]

        tmp = sb("tmp", [P, 2, T], F32, at_scratch)
        var = sb("var", [P, T], F32, at_scratch + 4 * KB)
        rs = sb("rs", [P, T], F32, at_scratch + 6 * KB)
        rs_sq = sb("rs_sq", [P, T], F32, at_scratch + 8 * KB)
        c_rows = sb("c_rows", [P, D], F32, at_scratch + 12 * KB)
        h_raw = sb("h_raw", [P, 4, T], F32, at_scratch + 4 * KB)
        urow = sb("urow", [P, ROW], F32, at_scratch + 10 * KB)
        wsum = [sb(f"wsum{n}", [P, ROW], F32, at_scratch + 10 * KB + (n + 1) * 4 * ROW) for n in range(2)]
        sig0 = sb("sig0", [P, T], F32, at_scratch + 10 * KB + 3 * 4 * ROW)
        sq_a = sb("sq_a", [P, T], F32, at_scratch + 10 * KB)
        sq_b = sb("sq_b", [P, T], F32, at_scratch + 12 * KB)
        sum_a = sb("sum_a", [P, T], F32, at_scratch + 14 * KB)
        sum_b = sb("sum_b", [P, T], F32, at_scratch + 16 * KB)
        r_both = sb("r_both", [P, T], F32, at_scratch + 10 * KB)
        r_mem = sb("r_mem", [P, MEM], F32, at_scratch + 19 * KB)
        r_one = sb("r_one", [P, T], F32, at_scratch + 18 * KB)
        gate_sig = sb("gate_sig", [P, 3, T], F32, at_scratch + 10 * KB)
        part = sb("part", [P, 2, T], F32, at_scratch + 4 * KB)
        x_back = sb("x_back", [P, 2, T], F32, at_scratch + 10 * KB)
        result = sb("result", [P, 2, T], F32, at_scratch + 14 * KB)

        wmod_sb = [sb(f"wmod{n}", [P, D], F32, at_x2 + 8 * n * KB) for n in range(4)]
        front_raw = sb("front_raw", [P, 4, D], F32, at_x2 + 32 * KB)
        squares = sb("squares", [P, 4, T], F32, at_x1)
        mem_squares = sb("mem_squares", [P, KT, MEM], F32, at_x2 + 16 * KB)
        memn_hi = sb("memn_hi", [P, KT, MEM], F32R, at_x2 + 16 * KB)
        mem_raw = sb("mem_raw", [P, KT, MEM], F32, at_x2 + 32 * KB)
        memn_lo = sb("memn_lo", [P, KT, MEM], F32R, at_x2 + 32 * KB)
        c_rows3 = sb("c_rows3", [P, D], F32, at_x2 + 48 * KB)
        x_in = sb("x_in", [P, 2, T], F32, at_x2 + 56 * KB)
        msrc0 = sb("msrc0", [P, MEM], F32, at_x2 + 60 * KB)
        mem_out = sb("mem_out", [P, MEM], F32, at_x2 + 61 * KB)
        q_t = sb("q_t", [P, T], F32, at_x2)
        k_t = sb("k_t", [P, T], F32, at_x2 + 2 * KB)
        v_n = sb("v_n", [P, NB, P], F32, at_x2 + 4 * KB)
        z_exp = sb("z_exp", [P, T], F32, at_x2 + 6 * KB)
        z_t = sb("z_t", [P, T], F32, at_x2 + 8 * KB)
        msrc = sb("msrc", [P, T], F32, at_x2 + 10 * KB)
        probs = sb("probs", [P, 2, 10 * P], F32, at_x2 + 12 * KB)
        probs_t = sb("probs_t", [P, 2, 10 * P], F32, at_x2 + 22 * KB)
        neg_c = sb("neg_c", [P, 2, T], F32, at_x2 + 32 * KB)
        bias_a = sb("bias_a", [P, 2, 2 * P], F32, at_x2 + 36 * KB)
        dist_a = sb("dist_a", [P, 2 * P], F32, at_x2 + 38 * KB)
        zero_c = sb("zero_c", [P, MEM], F32, at_x2 + 39 * KB)
        plain = sb("plain", [P, T], F32, at_x2 + 46 * KB)
        f_a = sb("f_a", [P, T], F32, at_x2 + 40 * KB)
        f_b = sb("f_b", [P, T], F32, at_x2 + 42 * KB)
        f_c = sb("f_c", [P, T], F32, at_x2 + 44 * KB)

        bank = [ctx.enter_context(nc.psum_tensor(f"bank{n}", [P, T], F32)) for n in range(8)]
        acc = bank[0:2]
        score = bank[2:4]
        turned = bank[4:6]
        ctx_out = bank[6]
        misc = bank[7]

        consts_loaded, cols_loaded, mask_loaded = sem("consts_loaded"), sem("cols_loaded"), sem("mask_loaded")
        mem_loaded, c_loaded, dist_loaded = sem("mem_loaded"), sem("c_loaded"), sem("dist_loaded")
        x_loaded = [sem(f"x_part{n}_loaded") for n in range(4)]
        front_loaded = [sem(f"front_raw{n}_loaded") for n in range(4)]
        consts_ready, c_ready = sem("consts_ready"), sem("c_silu_ready")
        w_loaded = [sem(f"w_half{n}_loaded") for n in range(2)]
        hi_ready, lo_ready, w_used = sem("w_hi_ready"), sem("w_lo_ready"), sem("w_quarter_used")
        wmod_loaded, wmod_used = [sem(f"wmod{n}_loaded") for n in range(4)], sem("wmod_used")
        square_ready, square_used = sem("square_ready"), sem("square_used")
        var_ready, rs_ready = sem("var_ready"), sem("rs_ready")
        rx_ready, xr_ready = sem("rx_ready"), sem("xr_ready")
        mem_square_ready, mem_sum_full, memn_ready = sem("mem_square_ready"), sem("mem_sum_full"), sem("memn_ready")
        h_made, h_hi, h_ready = sem("h_made"), sem("h_high_ready"), sem("h_ready")
        hn_made, hn_hi = sem("hn_made"), sem("hn_high_ready")
        yz_hi, y_hi = sem("yz_high_ready"), sem("y_high_ready")
        acc_free = [sem(f"acc{n}_free") for n in range(2)]
        msrc_ready, misc_full, misc_free = sem("msrc_ready"), sem("misc_full"), sem("misc_free")
        mem_out_ready, mem_out_stored = sem("mem_out_ready"), sem("mem_out_stored")
        urow_zeroed, urow_ready, urow_used = sem("urow_zeroed"), sem("urow_ready"), sem("urow_used")
        sig_ready, sig_used = sem("sig_ready"), sem("sig_used")
        pooled_ready, yg_ready = sem("pooled_ready"), sem("yg_ready")
        x_in_loaded, gate_c_loaded = [sem(f"x_in{n}_loaded") for n in range(2)], sem("gate_c_loaded")
        x1_ready, sq_ready, sq_added = sem("x1_ready"), sem("square_pair_ready"), sem("square_pair_added")
        sums_zeroed, sums_full = sem("sums_zeroed"), sem("sums_full")
        hn_ready, xp_ready = sem("hn_ready"), sem("x_prime_ready")
        xp_stored = [sem(f"x_prime{n}_stored") for n in range(2)]
        f_abs, f_ln, c_neg_ready, c_stored = sem("f_abs_ready"), sem("f_ln_ready"), sem("c_neg_ready"), sem("c_stored")
        neg_c_loaded = [sem(f"neg_c{n}_loaded") for n in range(2)]
        k_loaded, v_loaded = sem("k_loaded"), sem("v_loaded")
        q_ready, k_ready, v_ready = sem("q_ready"), sem("k_ready"), sem("v_ready")
        plain_ready, plain_used = sem("plain_ready"), sem("plain_used")
        z_exp_ready, z_ready = sem("z_exp_ready"), sem("z_ready")
        score_full, score_read = sem("score_full"), sem("score_read")
        exp_done, sink_done, rden_ready = sem("exp_done"), sem("sink_exp_done"), sem("rden_ready")
        probs_ready, turned_full, turned_copied = sem("probs_ready"), sem("turned_full"), sem("turned_copied")
        pv_done, ctx_free = sem("pv_done"), sem("ctx_free")
        yz_ready, gsig_ready, branch_part = sem("yz_split"), sem("gate_sig_ready"), sem("branch_part")
        y_ready, y_split = sem("y_ready"), sem("y_split")
        x_back_loaded = [sem(f"x_back{n}_loaded") for n in range(2)]
        result_ready, result_stored = sem("result_ready"), [sem(f"result{n}_stored") for n in range(2)]

        from_one = [*acc_free, ctx_free, misc_free, misc_full, pv_done, *result_stored,
                       score_read, sig_used, sq_added, turned_copied]

        TOTAL = 4 * PANELS

        def load_panel(sp, g):
            srcs = [stream[g.pick(), :, half * 8 * P:(half + 1) * 8 * P].rearrange("a p n -> p (a n)") for half in range(2)]
            for half, src in enumerate(srcs):
                if g.lowest() > FRONT:
                    sp.wait_ge(lo_ready, ((g - 1).times(4) + (2 * half + 2)).value())
                sp.dma_start(w_raw[:, half, :], src).then_inc(w_loaded[half], 16)

        def raw_quarter(s):
            if s.lowest() < 4 * FRONT:
                return front_raw[:, s.c // 4 % 4, s.c % 4 * 4 * P:(s.c % 4 + 1) * 4 * P]
            return w_raw[:, s.c % 4 // 2, s.c % 2 * 4 * P:(s.c % 2 + 1) * 4 * P]

        def split_hi(act, t):
            s = t + 3
            act.drain()
            if s.i is None and s.c >= TOTAL:
                return
            q = s.c % 4
            if s.lowest() < 4 * FRONT:
                act.wait_ge(front_loaded[s.c // 4 % 4], 16 * (s.c // 16 + 1))
            else:
                g = At(s.c // 4, s.k // 4, s.i)
                act.wait_ge(w_loaded[q // 2], (g - (FRONT - 1)).times(16).value())
            if (s - 3).positive():
                act.wait_ge(w_used, (s - 3).value())
            nc.scalar.activation(w_hi[:, q, :], raw_quarter(s), ACT.Copy).then_inc(hi_ready, 1)

        def split_lo(dve, t):
            s = t + 3
            dve.drain()
            if s.i is None and s.c >= TOTAL:
                return
            q = s.c % 4
            dve.wait_ge(hi_ready, (s + 1).value())
            nc.vector.tensor_tensor(w_lo[:, q, :], raw_quarter(s), w_hi[:, q, :].bitcast(F32),
                                    ALU.subtract).then_inc(lo_ready, 1)

        def tile_products(bank_ap, q, k, x_hi, x_lo, kx, start, stop, tokens=T):
            hi, lo = w_hi[:, q, k * P:(k + 1) * P], w_lo[:, q, k * P:(k + 1) * P]
            nc.tensor.matmul(bank_ap[:, :tokens], hi, x_hi[:, kx, :], start=start, stop=False)
            nc.tensor.matmul(bank_ap[:, :tokens], hi, x_lo[:, kx, :], start=False, stop=False)
            return nc.tensor.matmul(bank_ap[:, :tokens], lo, x_hi[:, kx, :], start=False, stop=stop)

        def panel(pe, g, r, x_hi, x_lo, between=None, tokens=T, ready=None):
            pe.wait_ge(acc_free[r.parity()], (r.half() + ONE).value())
            for q in range(4):
                if between and q in between:
                    between[q]()
                if ready is not None:
                    pe.wait_ge(ready, 4 * (q + 1))
                t = g.times(4) + q
                pe.wait_ge(lo_ready, (t + 1).value())
                for k in range(4):
                    mm = tile_products(acc[r.parity()], q, k, x_hi, x_lo, 4 * q + k, q == 0 and k == 0,
                                       q == 3 and k == 3, tokens)
                mm.then_inc(w_used, 1)

        def rstd_guess(act, width, m):
            act.wait_ge(var_ready, (m + 1).value())
            nc.scalar.activation(rs[:, :width], var[:, :width], ACT.Ln)
            act.drain()
            nc.scalar.activation(rs[:, :width], rs[:, :width], ACT.Exp, scale=-0.5)
            act.drain()
            nc.scalar.activation(rs_sq[:, :width], rs[:, :width], ACT.Square).then_inc(rs_ready, 1)

        def rstd_newton(dve, dst, width, m):
            dve.wait_ge(rs_ready, (m + 1).value())
            nc.vector.scalar_tensor_tensor(rs_sq[:, :width], rs_sq[:, :width], -0.5, var[:, :width], ALU.mult, ALU.mult)
            dve.drain()
            nc.vector.scalar_tensor_tensor(dst, rs_sq[:, :width], 1.5, rs[:, :width], ALU.add, ALU.mult)
            dve.drain()

        def split_act(dve, src, hi, lo, ready):
            dve.drain()
            nc.vector.tensor_copy(hi, src)
            dve.drain()
            nc.vector.tensor_tensor(lo, src, hi.bitcast(F32), ALU.subtract).then_inc(ready, 1)
            dve.drain()

        def tile(x, n):
            return x[:, n.pick(), :].rearrange("p a t -> p (a t)")

        LEN = {"b": [P * (n + 1) for n in range(NB)], "a": [P] + [2 * P] * (NB - 1), "c": [MEM] * NB}
        KEY0 = {"b": [0] * NB, "a": [0] + [P * n for n in range(NB - 1)], "c": [0] * NB}
        OFF = {kind: [sum(LEN[kind][:n]) for n in range(NB)] for kind in LEN}

        def rows_of(kind, slot):
            return slice(0, P) if kind == "c" else slice(HEAD * slot, HEAD * slot + HEAD)

        class Attention:

            def __init__(self, kind, job, keys):
                self.kind, self.job, self.keys = kind, job, keys
                self.heads = 1 if kind == "c" else 2
                self.head = At(job.c + 12, job.k, job.i) if kind == "c" else job.times(2)
                self.done = self.head + self.heads
                self.tile = job + {"a": -6, "b": 6, "c": 0}[kind]

        class Window:

            def __init__(self, g, r, first, prev=None, prev_n=None, misc_n=None, rs_n=None, out_n=None,
                         attention=None, biased=None, loads=None, extra=None, scale=None):
                self.g, self.r, self.t = g, r, g.times(4)
                self.first, self.prev, self.prev_n = first, prev, prev_n
                self.misc_n, self.rs_n, self.out_n = misc_n, rs_n, out_n
                self.attention, self.biased, self.loads, self.extra, self.scale = attention, biased, loads, extra, scale

        def pe_scores(pe, at, slot, half):
            rows, head = rows_of(at.kind, slot), at.head + slot
            if slot == 0 and half == 0:
                pe.wait_ge(q_ready, (at.job + 1).value())
                if at.kind == "c":
                    pe.wait_ge(k_loaded, (at.keys.times(16)).value())
                else:
                    pe.wait_ge(k_ready, at.keys.value())
            for n in (2 * half, 2 * half + 1):
                pe.wait_ge(score_read, (head.times(4) + n + ONE).value())
                width, k0 = LEN[at.kind][n], KEY0[at.kind][n]
                mm = nc.tensor.matmul(score[n % 2][:, :width], q_t[rows, n * P:(n + 1) * P],
                                      k_t[rows, k0:k0 + width], start=True, stop=True)
                if at.kind == "b":
                    mm = nc.tensor.matmul(score[n % 2][:, width - P:width], ident_b[:, :], causal_b[:, :],
                                          start=False, stop=True, skip_group_check=True)
                mm.then_inc(score_full, 1)

        def pe_turn(pe, at, slot, half):
            head = at.head + slot
            for n in (2 * half, 2 * half + 1):
                pe.wait_ge(probs_ready, (head.times(4) + (n + 1)).value())
                pe.wait_ge(turned_copied, (head.times(4) + n + ONE).value())
                for kb in range(LEN[at.kind][n] // P):
                    o = OFF[at.kind][n] + kb * P
                    mm = nc.tensor.transpose(turned[n % 2][:, kb * P:(kb + 1) * P], probs[:, slot, o:o + P], ident[:, :])
                mm.then_inc(turned_full, 1)

        def pe_values(pe, at, slot):
            rows, head = rows_of(at.kind, slot), at.head + slot
            if slot == 0:
                pe.wait_ge(ctx_free, (at.job + ONE).value())
                if at.kind == "c":
                    pe.wait_ge(v_loaded, (at.keys.times(16)).value())
                else:
                    pe.wait_ge(v_ready, at.keys.value())
            for n in range(NB):
                pe.wait_ge(turned_copied, (head.times(4) + (n + 2) + ONE).value())
                count = LEN[at.kind][n] // P
                for kb in range(count):
                    o = OFF[at.kind][n] + kb * P
                    mm = nc.tensor.matmul(ctx_out[rows, n * P:(n + 1) * P], v_n[:, KEY0[at.kind][n] // P + kb, rows],
                                          probs_t[:, slot, o:o + P], start=kb == 0, stop=kb == count - 1)
            mm.then_inc(pv_done, 1)

        def pe_squares(pe, source, weights, width, m):
            pe.wait_ge(msrc_ready, (m + 1).value())
            pe.wait_ge(misc_free, (m + ONE).value())
            nc.tensor.matmul(misc[:, :width], weights[:, :], source[:, :width], start=True, stop=True).then_inc(misc_full, 1)

        def pe_turn_values(pe, source, width, m):
            pe.wait_ge(msrc_ready, (m + 1).value())
            pe.wait_ge(misc_free, (m + ONE).value())
            for kb in range(width // P):
                mm = nc.tensor.transpose(misc[:, kb * P:(kb + 1) * P], source[:, kb * P:(kb + 1) * P], ident[:, :])
            mm.then_inc(misc_full, 1)

        def pe_window(pe, w):
            at = w.attention
            two = at is not None and at.heads == 2

            def before_1():
                if at:
                    pe_scores(pe, at, 0, 0)

            def before_2():
                if at:
                    pe_scores(pe, at, 0, 1)
                if w.prev == "v":
                    pe_turn_values(pe, msrc, T, w.misc_n)

            def before_3():
                if two:
                    pe_scores(pe, at, 1, 0)

            def before_4():
                if two:
                    pe_scores(pe, at, 1, 1)

            def before_5():
                if at:
                    pe_turn(pe, at, 0, 0)

            def before_6():
                if at:
                    pe_turn(pe, at, 0, 1)
                if w.first != "gate":
                    pe_squares(pe, msrc, ones if w.first == "qc" else blocks, T, w.misc_n + (w.prev == "v"))

            def before_7():
                if at:
                    pe_values(pe, at, 0)
                if two:
                    pe_turn(pe, at, 1, 0)

            panel(pe, w.g, w.r, x1_hi, x1_lo, {1: before_1, 2: before_2, 3: before_3})
            panel(pe, w.g + 1, w.r + 1, x1_hi, x1_lo, {0: before_4, 1: before_5, 2: before_6, 3: before_7})
            if two:
                pe_turn(pe, at, 1, 1)
            if two:
                pe_values(pe, at, 1)

        def act_exp(act, at, slot, half):
            head = at.head + slot
            for n in (2 * half, 2 * half + 1):
                c = 4 * slot + n
                act.wait_ge(score_read, (head.times(4) + (n + 2) + ONE).value())
                seg = probs[:, slot, OFF[at.kind][n]:OFF[at.kind][n] + LEN[at.kind][n]]
                nc.scalar.activation(seg, seg, ACT.Exp, bias=neg_max[:, c:c + 1], scale=-1.0,
                                     accum_out=den[:, c:c + 1]).then_inc(exp_done, 1)
            if at.kind == "a" and half == 1:
                nc.scalar.activation(sink_exp[:, 4 * slot:4 * slot + 4], neg_max[:, 4 * slot:4 * slot + 4], ACT.Exp,
                                     bias=sink_col[:, slot:slot + 1]).then_inc(sink_done, 1)

        def act_turned(act, at, slot, half):
            head = at.head + slot
            if half == 0:
                act.wait_ge(pv_done, (at.head + ONE).value())
            for n in (2 * half, 2 * half + 1):
                act.wait_ge(turned_full, (head.times(4) + (n + 1)).value())
                o, width = OFF[at.kind][n], LEN[at.kind][n]
                nc.scalar.activation(probs_t[:, slot, o:o + width], turned[n % 2][:, :width], ACT.Copy).then_inc(turned_copied, 1)

        def act_window(act, w):
            at = w.attention
            two = at is not None and at.heads == 2
            for s in range(8):
                t = w.t + s
                split_hi(act, t)
                if s == 0 and w.prev == "v":
                    act.wait_ge(w_used, t.value())
                    act.wait_ge(misc_full, (w.misc_n + ONE).value())
                    nc.scalar.activation(msrc[:, :], acc[(w.r - 1).parity()][:, :], ACT.Copy).then_inc(msrc_ready, 1)
                    act.drain().then_inc(acc_free[(w.r - 1).parity()], 1)
                if s == 0 and w.prev == "z":
                    act.wait_ge(w_used, t.value())
                    act.wait_ge(ctx_free, (w.prev_n + ONE).value())
                    before = acc[(w.r - 1).parity()]
                    nc.scalar.activation(z_exp[:, :], before[:, :], ACT.Exp, scale=-1.0)
                    nc.scalar.activation(z_t[:, :], before[:, :], ACT.Copy).then_inc(z_exp_ready, 1)
                    act.drain().then_inc(acc_free[(w.r - 1).parity()], 1)
                if s == 1 and w.prev == "f":
                    act.wait_ge(f_abs, 1)
                    nc.scalar.activation(f_c[:, :], f_b[:, :], ACT.Exp, scale=-1.0)
                    act.drain()
                    nc.scalar.activation(f_c[:, :], f_c[:, :], ACT.Ln, bias=1.0).then_inc(f_ln, 1)
                if s in (1, 2) and at:
                    act_exp(act, at, 0, s - 1)
                if s in (3, 4) and two:
                    act_exp(act, at, 1, s - 3)
                if s == 4 and w.first != "gate":
                    act.wait_ge(w_used, t.value())
                    act.wait_ge(misc_full, (w.misc_n + (w.prev == "v") + ONE).value())
                    if (w.rs_n - 8).positive():
                        act.wait_ge(plain_used, (w.rs_n - 8).value())
                    nc.scalar.activation(msrc[:, :], acc[w.r.parity()][:, :], ACT.Square).then_inc(msrc_ready, 1)
                    nc.scalar.activation(plain[:, :], acc[w.r.parity()][:, :], ACT.Copy).then_inc(plain_ready, 1)
                    act.drain().then_inc(acc_free[w.r.parity()], 1)
                if s == 4 and w.first == "gate":
                    act_gate(act, w.r, t, 0, w.out_n)
                if s in (5, 6) and at:
                    act_turned(act, at, 0, s - 5)
                if s == 6 and w.first != "gate":
                    rstd_guess(act, T, w.rs_n)
                if s == 7 and two:
                    act_turned(act, at, 1, 0)
                    act_turned(act, at, 1, 1)

        def act_gate(act, r, t, b, n):
            act.wait_ge(w_used, t.value())
            if n.positive():
                act.wait_ge(y_ready, n.value())
            nc.scalar.activation(gate_sig[:, b, :], acc[r.parity()][:, :], ACT.Sigmoid).then_inc(gsig_ready, 1)
            act.drain().then_inc(acc_free[r.parity()], 1)

        def dve_scores(dve, at, slot, half):
            head = at.head + slot
            dve.drain()
            if at.kind == "b" and half == 0:
                dve.wait_ge(neg_c_loaded[slot], (at.job + 1).times(16).value())
            for n in (2 * half, 2 * half + 1):
                width = LEN[at.kind][n]
                dve.wait_ge(score_full, (head.times(4) + (n + 1)).value())
                if at.kind == "a":
                    bias, most = bias_a[:, slot, 2 * P - width:], neg_sink[:, slot:slot + 1]
                else:
                    bias, most = (neg_c[:, slot, :width] if at.kind == "b" else zero_c[:, :]), 3e38
                c = 4 * slot + n
                nc.vector.memset(arrived[:, c:c + 1], 0.0)
                nc.vector.tensor_tensor_reduce(
                    out=probs[:, slot, OFF[at.kind][n]:OFF[at.kind][n] + width], in0=score[n % 2][:, :width], in1=bias,
                    scale=-1.0, scalar=most, op0=ALU.add, op1=ALU.min, accum_out=neg_max[:, c:c + 1]).then_inc(score_read, 1)

        def dve_denominator(dve, at, slot):
            head = at.head + slot
            dve.wait_ge(exp_done, (head.times(4) + 4).value())
            seg = slice(4 * slot, 4 * slot + 4)
            if at.kind == "a":
                dve.wait_ge(sink_done, (head - 11).value())
                nc.vector.tensor_tensor(den[:, seg], den[:, seg], sink_exp[:, seg], ALU.add)
                dve.drain()
            nc.vector.reciprocal(rden[:, seg], den[:, seg]).then_inc(rden_ready, 1)

        def dve_window(dve, w):
            at = w.attention
            two = at is not None and at.heads == 2
            before = acc[(w.r - 1).parity()]
            for s in range(8):
                t = w.t + s
                split_lo(dve, t)
                if w.extra:
                    w.extra(s)
                if s == 0 and w.prev == "f":
                    dve.wait_ge(w_used, t.value())
                    nc.vector.tensor_scalar(f_a[:, :], before[:, :], col("b_forget"), None, ALU.add)
                    dve.drain().then_inc(acc_free[(w.r - 1).parity()], 1)
                    nc.vector.scalar_tensor_tensor(f_b[:, :], f_a[:, :], -1.0, f_a[:, :], ALU.mult, ALU.max).then_inc(f_abs, 1)
                if s == 2 and w.prev == "f":
                    dve.wait_ge(f_ln, 1)
                    nc.vector.tensor_scalar(f_a[:, :], f_a[:, :], 0.0, None, ALU.min)
                    dve.drain()
                    nc.vector.tensor_tensor(f_b[:, :], f_c[:, :], f_a[:, :], ALU.subtract)
                    dve.drain()
                if 3 <= s < 6 and w.prev == "f":
                    for step in range(3 * (s - 3), 3 * (s - 2)):
                        a, b = (f_b, f_a) if step % 2 == 0 else (f_a, f_b)
                        n = 1 << step
                        nc.vector.tensor_copy(b[:HEADS_B, :n], a[:HEADS_B, :n])
                        ins = nc.vector.tensor_tensor(b[:HEADS_B, n:], a[:HEADS_B, n:], a[:HEADS_B, :T - n], ALU.add)
                        if n == T // 2:
                            ins.then_inc(c_neg_ready, 1)
                        dve.drain()
                if s in (1, 2) and at:
                    dve_scores(dve, at, 0, s - 1)
                if s == 2 and w.prev == "v":
                    dve.wait_ge(misc_full, (w.misc_n + 1 + ONE).value())
                    nc.vector.tensor_copy(v_n[:, :, :].rearrange("p b d -> p (b d)"), misc[:, :]).then_inc(v_ready, 1)
                    dve.drain().then_inc(misc_free, 1)
                if s == 2 and w.prev == "z":
                    dve.wait_ge(z_exp_ready, (w.prev_n + 1).value())
                    nc.vector.tensor_scalar(z_exp[:, :], z_exp[:, :], 1.0, None, ALU.add)
                    dve.drain()
                    nc.vector.reciprocal(z_exp[:, :T // 2], z_exp[:, :T // 2])
                if s in (3, 4) and two:
                    dve_scores(dve, at, 1, s - 3)
                if s == 3 and at:
                    dve_denominator(dve, at, 0)
                if s == 5 and two:
                    dve_denominator(dve, at, 1)
                if s == 4 and w.prev == "z":
                    nc.vector.reciprocal(z_exp[:, T // 2:], z_exp[:, T // 2:])
                if s == 5 and w.prev == "z":
                    dve.drain()
                    nc.vector.tensor_tensor(z_t[:, :], z_t[:, :], z_exp[:, :], ALU.mult).then_inc(z_ready, 1)
                if s == 5 and w.biased is not None:
                    for slot in range(2):
                        n = (w.biased - 6).times(2) + slot
                        nc.vector.tensor_scalar(bias_a[:, slot, :], dist_a[:, :], slopes[:, n.pick()], None, ALU.mult)
                        nc.vector.tensor_copy(sink_col[:, slot:slot + 1], col("sinks", n))
                    dve.drain()
                    nc.vector.tensor_scalar(neg_sink[:, :], sink_col[:, :], -1.0, None, ALU.mult)
                if s == 6 and w.first != "gate":
                    m = w.misc_n + (w.prev == "v")
                    dve.wait_ge(misc_full, (m + 1 + ONE).value())
                    nc.vector.tensor_scalar(var[:, :], misc[:, :], 1.0 / (P if w.first == "qc" else HEAD), EPS,
                                            ALU.mult, ALU.add).then_inc(var_ready, 1)
                    dve.drain().then_inc(misc_free, 1)
                if s == 7 and w.first != "gate":
                    rstd_newton(dve, rs[:, :], T, w.rs_n)
                    dst, ready, gain = {"kb": (k_t, k_ready, "kg_b"), "ka": (k_t, k_ready, "kg_a"),
                                        "qb": (q_t, q_ready, "qg_b"), "qa": (q_t, q_ready, "qg_a"),
                                        "qc": (q_t, q_ready, "qg_c")}[w.first]
                    dve.wait_ge(plain_ready, (w.rs_n - 7).value())
                    nc.vector.scalar_tensor_tensor(dst[:, :], plain[:, :], col(gain), rs[:, :],
                                                   ALU.mult, ALU.mult).then_inc(ready, 1)
                    dve.drain().then_inc(plain_used, 1)
            if at:
                dve.drain()
                dve.wait_ge(pv_done, (at.done + ONE).value())
                nc.vector.tensor_tensor(tile(x3, at.tile), ctx_out[:, :], z_t[:, :], ALU.mult).then_inc(ctx_free, 1)

        def pool_window(pool, w):
            at = w.attention
            if at:
                for slot in range(at.heads):
                    head = at.head + slot
                    pool.wait_ge(rden_ready, (head + 1).value())
                    for n in range(NB):
                        seg = probs[:, slot, OFF[at.kind][n]:OFF[at.kind][n] + LEN[at.kind][n]]
                        by = rden[:, 4 * slot + n:4 * slot + n + 1].to_broadcast([P, LEN[at.kind][n]])
                        nc.gpsimd.tensor_tensor(seg, seg, by, ALU.mult).then_inc(probs_ready, 1)
            if w.loads is None:
                return
            kind, n = w.loads
            if kind == "b":
                pool.wait_ge(score_read, (n.times(8) + 1 + ONE).value())
                for slot in range(2):
                    row = n.times(2) + slot
                    pool.dma_start(neg_c[:, slot, :], c_store[row.pick(), :].to_broadcast([P, T])).then_inc(neg_c_loaded[slot], 16)
            else:
                pool.wait_ge(pv_done, (n + 24 + ONE).value())
                pool.dma_start(k_t[:, :MEM], mkv_store[n.pick(), :, :].rearrange("a p t -> p (a t)")).then_inc(k_loaded, 16)
                pool.dma_start(v_n[:, :2, :].rearrange("p b d -> p (b d)"),
                               mkv_store[(n + HEADS_C).pick(), :, :].rearrange("a p t -> p (a t)")).then_inc(v_loaded, 16)

        def windows(eng, run, extra=None):
            gb, rb, ga, ra, gc, rc = (FIRST["b"], RESULT["b"], FIRST["a"], RESULT["a"], FIRST["c"], RESULT["c"])

            def b_keys(j, attention):
                run(eng, Window(At(gb + 4 * j.c, 4 * j.k, j.i), At(rb + 4 * j.c, 4 * j.k, j.i),
                                "kb", "z" if attention else "f", j - 1, j.times(3) + 8, j.times(2) + 8,
                                attention=attention, extra=extra if attention is None else None))

            def b_queries(j, more=None):
                run(eng, Window(At(gb + 2 + 4 * j.c, 4 * j.k, j.i), At(rb + 2 + 4 * j.c, 4 * j.k, j.i),
                                "qb", "v", None, j.times(3) + 9, j.times(2) + 9, loads=("b", j), extra=more))

            b_keys(At(0), None)
            b_queries(At(0), (lambda s: extra(s + 8)) if extra else None)
            with steps(eng, 1, HEADS_B // 2) as i:
                j = At(0, 1, i)
                b_keys(j, Attention("b", j - 1, j))
                b_queries(j)
            for c in range(2):
                g, r, m = ga + 8 * c, ra + 8 * c, 26 + 5 * c
                last = Attention("b", At(5), At(6)) if c == 0 else Attention("a", At(8), At(7))
                run(eng, Window(At(g), At(r), "ka", "z", At(5 + 3 * c), At(m), At(20 + 4 * c), attention=last))
                run(eng, Window(At(g + 2), At(r + 2), "qa", "v", None, At(m + 1), At(21 + 4 * c), biased=At(6 + 3 * c)))
                with steps(eng, 1, GROUPS) as i:
                    job = At(6 + 3 * c, 1, i)
                    run(eng, Window(At(g + 2, 2, i), At(r + 2, 2, i), "qa", "z", job - 1, At(m + 2, 1, i),
                                    At(21 + 4 * c, 1, i), attention=Attention("a", job - 1, At(7 + c)), biased=job))
            run(eng, Window(At(gc), At(rc), "qc", "z", At(11), At(36), At(28), attention=Attention("a", At(11), At(8)),
                            loads=("c", At(0))))
            with steps(eng, 1, HEADS_C) as i:
                run(eng, Window(At(gc, 2, i), At(rc, 2, i), "qc", "z", At(11, 1, i), At(36, 1, i), At(28, 1, i),
                                attention=Attention("c", At(11, 1, i), At(0, 1, i)), loads=("c", At(0, 1, i))))
            run(eng, Window(At(FIRST["gated"]), At(RESULT["gated"]), "gate", "z", At(15), out_n=At(0),
                            attention=Attention("c", At(15), At(4))))

        def mem_kind(n):
            return None if n == 0 else "k" if n <= HEADS_C else "v"

        block = ctx.enter_context(nc.Block())

        @block.sync
        def _(sp):
            for name, dst in (("ident", ident), ("ones", ones), ("blocks", blocks), ("slopes", slopes)):
                a, b = CONST[name]
                sp.dma_start(dst[:, :], const_in[:, a:b]).then_inc(consts_loaded, 16)
            a, b = CONST["edges"]
            sp.dma_start(edges[:, :, :].rearrange("p a b -> p (a b)"), const_in[:, a:b]).then_inc(consts_loaded, 16)
            a, b = CONST["causal"]
            sp.dma_start(tmp[:, 1, :P], const_in[:, a:b]).then_inc(mask_loaded, 16)
            sp.dma_start(cols[:, :], cols_in).then_inc(cols_loaded, 16)
            for m in range(2 * KT):
                row = (m % 2 * KT + m // 2) * P
                if m >= 4:
                    sp.wait_ge(wmod_used, m - 3)
                sp.dma_start(wmod_sb[m % 4][:, :], wmod[row:row + P, :]).then_inc(wmod_loaded[m % 4], 16)
                if m % 4 == 3:
                    panel_n = m // 4
                    if panel_n >= 4:
                        sp.wait_ge(lo_ready, 4 * (panel_n - 3))
                    sp.dma_start(front_raw[:, panel_n % 4, :], stream[panel_n, :, :]).then_inc(front_loaded[panel_n % 4], 16)
            load_panel(sp, At(FRONT))
            with steps(sp, FRONT + 1, FIRST["pool_out"]) as i:
                load_panel(sp, At(0, 1, i))
            def end_loads(m, slot, again=True):
                gate_rows, x_rows = wmod[(m.times(P) + 2 * KT * P).pick(P), :], xT[m.times(P).pick(P), :]
                load_panel(sp, m + FIRST["pool_out"])
                if not again and slot == 0:
                    sp.wait_ge(w_used, 4 * FIRST["pool_out"])
                    sp.dma_start(mem_raw[:, :, :], memT.rearrange("(k p) t -> p k t", p=P)).then_inc(mem_loaded, 16)
                if again:
                    sp.wait_ge(wmod_used, (m + (2 * KT - 1)).value())
                sp.dma_start(wmod_sb[slot][:, :], gate_rows).then_inc(wmod_loaded[slot], 16)
                if again:
                    sp.wait_ge(x1_ready, (m - 1).value())
                sp.dma_start(x_in[:, slot, :], x_rows).then_inc(x_in_loaded[slot], 16)
            for slot in range(2):
                end_loads(At(slot), slot, again=False)
            with steps(sp, 1, KT // 2) as i:
                for slot in range(2):
                    end_loads(At(slot, 2, i), slot)
            with steps(sp, FIRST["mem"], FIRST["out"]) as i:
                load_panel(sp, At(0, 1, i))
            def back_loads(n, slot, again=True):
                src = x_store[n.pick(), :, :].rearrange("a p t -> p (a t)")
                load_panel(sp, n + FIRST["out"])
                if again:
                    sp.wait_ge(result_ready, (n - 1).value())
                else:
                    sp.wait_ge(xp_stored[slot], 16 * KT // 2)
                    sp.wait_ge(y_ready, KT)
                sp.dma_start(x_back[:, slot, :], src).then_inc(
                    x_back_loaded[slot], 16)
            for slot in range(2):
                back_loads(At(slot), slot, again=False)
            with steps(sp, 1, KT // 2) as i:
                for slot in range(2):
                    back_loads(At(slot, 2, i), slot)

        @block.tensor
        def _(pe):
            pe.wait_ge(consts_loaded, 16 * 5)
            for k in range(KT):
                pe.wait_ge(square_ready, k + 1)
                nc.tensor.matmul(score[1][:, :], ones[:, :], squares[:, k % 4, :],
                                 start=k == 0, stop=k == KT - 1).then_inc(square_used, 1)

            for j in range(4):
                pe.wait_ge(h_ready, 4 * (j + 1))
                for o in range(FRONT):
                    pe.wait_ge(lo_ready, FRONT * j + o + 1)
                    for k in range(4):
                        mm = tile_products(bank[o], o % 4, k, x1_hi, x1_lo, 4 * j + k, j == 0 and k == 0,
                                           j == 3 and k == 3)
                    mm.then_inc(w_used, 1)
            g, r = FIRST["pool_in"], RESULT["pool_in"]
            with steps(pe, FRONT // 2, KT) as i:
                panel(pe, At(g, 2, i), At(r, 2, i), x1_hi, x1_lo)
                panel(pe, At(g + 1, 2, i), At(r + 1, 2, i), x1_hi, x1_lo)
            for grp in range(4):
                pe.wait_ge(pooled_ready, 4 * grp + 4)
                for q in range(4):
                    r = At(RESULT["group"] + 4 * grp + q)
                    pe.wait_ge(acc_free[r.parity()], (r.half() + ONE).value())
                    pe.wait_ge(lo_ready, 4 * (FIRST["group"] + grp) + q + 1)
                    for k in range(4):
                        mm = tile_products(acc[r.parity()], q, k, x2_hi, x2_lo, 4 * grp + k, k == 0, k == 3)
                    mm.then_inc(w_used, 1)
            g, r = FIRST["pool_out"], RESULT["pool_out"]
            panel(pe, At(g), At(r), x1_hi, x1_lo, ready=yg_ready)
            panel(pe, At(g + 1), At(r + 1), x1_hi, x1_lo)

            def mem_sum():
                for k in range(KT):
                    pe.wait_ge(mem_square_ready, k + 1)
                    mm = nc.tensor.matmul(score[0][:, :MEM], ones[:, :], mem_squares[:, k, :],
                                          start=k == 0, stop=k == KT - 1)
                mm.then_inc(mem_sum_full, 1)
            panel(pe, At(g + 2), At(r + 2), x1_hi, x1_lo, {3: mem_sum})
            panel(pe, At(g + 3), At(r + 3), x1_hi, x1_lo)
            with steps(pe, 2, KT // 2) as i:
                for n in range(2):
                    panel(pe, At(g + n, 2, i), At(r + n, 2, i), x1_hi, x1_lo)

            def x1_sums():
                pe.wait_ge(sq_added, 2 * KT + ONE)
                for which, total in ((0, sum_a), (1, sum_b)):
                    nc.tensor.matmul(score[which][:, :], ones[:, :], total[:, :], start=True, stop=True).then_inc(sums_full, 1)

            for n in range(2 * HEADS_C):
                def later():
                    if mem_kind(n) == "k":
                        pe_squares(pe, msrc0, ones, MEM, At(n - 1))
                    if mem_kind(n) == "v":
                        pe_turn_values(pe, msrc0, MEM, At(n - 1))
                between = {2: later}
                if n == 0:
                    pe.wait_ge(memn_ready, KT)
                if n == 1:
                    between[3] = x1_sums
                panel(pe, At(FIRST["mem"] + n), At(RESULT["mem"] + n), memn_hi, memn_lo, between, tokens=MEM)
            pe_turn_values(pe, msrc0, MEM, At(2 * HEADS_C - 1))
            panel(pe, At(FIRST["forget"]), At(RESULT["forget"]), x1_hi, x1_lo, ready=hn_ready)
            windows(pe, pe_window)

            def branches(g, r, ready=None):
                tiles = HEADS_A * HEAD // P, HEADS_B * HEAD // P, HEADS_C
                ends = [sum(tiles[:n + 1]) for n in range(3)]
                for q in range(4):
                    if ready is not None:
                        pe.wait_ge(ready, 4 * (q + 1))
                    pe.wait_ge(lo_ready, (g.times(4) + (q + 1)).value())
                    for k in range(4):
                        kk = 4 * q + k
                        b = sum(kk >= e for e in ends)
                        first = kk == 0 or kk in ends
                        if first:
                            pe.wait_ge(acc_free[(r + b).parity()], ((r + b).half() + ONE).value())
                        mm = tile_products(acc[(r + b).parity()], q, k, x2_hi, x2_lo, kk, first, kk + 1 in ends)
                    mm.then_inc(w_used, 1)
            g, r = FIRST["gated"], RESULT["gated"]
            panel(pe, At(g + 2), At(r + 2), x1_hi, x1_lo)
            branches(At(g + 3), At(r + 3), yz_ready)
            with steps(pe, 1, KT) as i:
                for b in range(3):
                    panel(pe, At(g + b, 4, i), At(r + b, 6, i), x1_hi, x1_lo)
                branches(At(g + 3, 4, i), At(r + 3, 6, i))
            g, r = FIRST["out"], RESULT["out"]
            panel(pe, At(g), At(r), x1_hi, x1_lo, ready=y_split)
            panel(pe, At(g + 1), At(r + 1), x1_hi, x1_lo)
            with steps(pe, 1, KT // 2) as i:
                for n in range(2):
                    panel(pe, At(g + n, 2, i), At(r + n, 2, i), x1_hi, x1_lo)

        @block.scalar
        def _(act):
            act.dma_start(c_rows[:, :], cvec.to_broadcast([P, D])).then_inc(c_loaded, 16)
            for n in range(4):
                act.dma_start(x3[:, 4 * n:4 * n + 4, :], xT[4 * n * P:4 * (n + 1) * P, :].rearrange(
                    "(k p) t -> p k t", p=P)).then_inc(x_loaded[n], 16)
            act.wait_ge(c_loaded, 16)
            nc.scalar.activation(c_rows[:, :], c_rows[:, :], ACT.Silu).then_inc(c_ready, 1)
            for k in range(KT):
                if k % 4 == 0:
                    act.wait_ge(x_loaded[k // 4], 16)
                if k >= 4:
                    act.wait_ge(square_used, k - 3)
                nc.scalar.activation(squares[:, k % 4, :], x3[:, k, :], ACT.Square).then_inc(square_ready, 1)
            rstd_guess(act, T, At(0))
            for q in range(3):
                split_hi(act, At(q - 3))
            for j in range(4):
                for k in range(4 * j, 4 * j + 4):
                    act.wait_ge(h_made, k + 1)
                    nc.scalar.activation(x1_hi[:, k, :], h_raw[:, k % 4, :], ACT.Copy).then_inc(h_hi, 1)
                for t in range(8 * j, 8 * j + 8):
                    split_hi(act, At(t))

            def sigmoid_of_g(n, source):
                act.wait_ge(sig_used, (n + ONE).value())
                nc.scalar.activation(sig0[:, :], source[:, :], ACT.Sigmoid).then_inc(sig_ready, 1)

            def row_of_u(n, source):
                if n.positive():
                    act.wait_ge(urow_used, n.value())
                nc.scalar.activation(urow[:, PAD:PAD + T], source[:, :], ACT.Copy).then_inc(urow_ready, 1)

            act.wait_ge(urow_zeroed, 1)

            def pool_in_beats(n, peeled=None):
                t = (n.times(2) + FIRST["pool_in"]).times(4)
                r = n.times(2) + RESULT["pool_in"]
                for s in range(8):
                    split_hi(act, t + s)
                    if peeled == 0 and s == 0:
                        act.wait_ge(w_used, 4 * FRONT)
                    if peeled == 0 and s % 2 == 0:
                        row_of_u(At(s // 2), bank[s])
                        if s == 0:
                            act.drain().then_inc(acc_free[0], 1)
                    if peeled == 0 and s % 2 == 1:
                        sigmoid_of_g(At(s // 2), bank[s])
                    if peeled != 0 and s == 0:
                        act.wait_ge(w_used, t.value())
                        if peeled == 1:
                            row_of_u(n - 1, acc[0])
                            act.drain().then_inc(acc_free[0], 1)
                        sigmoid_of_g(n - 1, acc[1])
                    if peeled != 0 and s == 4:
                        act.wait_ge(w_used, (t + 4).value())
                        row_of_u(n, acc[0])
                        act.drain().then_inc(acc_free[0], 1)
            pool_in_beats(At(FRONT // 2), peeled=0)
            pool_in_beats(At(FRONT // 2 + 1), peeled=1)
            with steps(act, FRONT // 2 + 2, KT) as i:
                pool_in_beats(At(0, 1, i))
            for n in range(KT):
                split_hi(act, At(4 * FIRST["group"] + n))
                if n == 0:
                    act.wait_ge(w_used, 4 * FIRST["group"])
                    sigmoid_of_g(At(KT - 1), acc[1])

            def squares_of_x1(m):
                act.wait_ge(x1_ready, (m + 1).value())
                act.wait_ge(sq_added, (m.times(2) + ONE).value())
                nc.scalar.activation(sq_a[:, :], tile(x3, m), ACT.Square).then_inc(sq_ready, 1)
                nc.scalar.activation(sq_b[:, :], tile(x3, m), ACT.Square, scale=col("final_g", m)).then_inc(sq_ready, 1)

            def pool_out_beat(m, peeled=False):
                t = (m + FIRST["pool_out"]).times(4)
                for s in range(4):
                    split_hi(act, t + s)
                    if peeled and s == 0:
                        act.wait_ge(w_used, t.value())
                        act.dma_start(c_rows3[:, :], cvec.to_broadcast([P, D])).then_inc(gate_c_loaded, 16)
                    if peeled and s == 2:
                        act.wait_ge(gate_c_loaded, 16)
                        nc.scalar.activation(c_rows3[:, :], c_rows3[:, :], ACT.Silu).then_inc(c_ready, 1)
                    if not peeled and s == 1:
                        squares_of_x1(m - 1)
                    if m.i is None and m.c == 1:
                        if s == 0:
                            act.wait_ge(mem_loaded, 16)
                        for k in range(4 * s, 4 * s + 4):
                            nc.scalar.activation(mem_squares[:, k, :], mem_raw[:, k, :], ACT.Square).then_inc(mem_square_ready, 1)
                    if m.i is None and m.c == 3 and s == 1:
                        rstd_guess(act, MEM, At(1))
            for m in range(4):
                pool_out_beat(At(m), peeled=m == 0)
                if m == 1:
                    act.preload_act_table_set("natural_log_exp_and_others")
            with steps(act, 2, KT // 2) as i:
                for slot in range(2):
                    pool_out_beat(At(slot, 2, i))

            def mem_source(n):
                act.wait_ge(w_used, 4 * (FIRST["mem"] + n))
                act.wait_ge(misc_full, n - 1 + ONE)
                before = acc[(n - 1) % 2][:, :MEM]
                kind = mem_kind(n)
                nc.scalar.activation(msrc0[:, :], before, ACT.Square if kind == "k" else ACT.Copy).then_inc(msrc_ready, 1)
                if kind == "v":
                    act.drain().then_inc(acc_free[(n - 1) % 2], 1)

            for n in range(2 * HEADS_C):
                for s in range(4):
                    split_hi(act, At(4 * (FIRST["mem"] + n) + s))
                    if n == 0 and s == 1:
                        squares_of_x1(At(KT - 1))
                    if n > 0 and s == 0:
                        mem_source(n)
                    if mem_kind(n) == "k" and s == 2:
                        rstd_guess(act, MEM, At(2 if n == 1 else n + 3))
                    if n == 1 and s == 3:
                        rstd_guess(act, T, At(3))
                    if n == 2 and s == 0:
                        rstd_guess(act, T, At(4))
                    if 3 <= n < 7:
                        k = 4 * (n - 3) + s
                        act.wait_ge(hn_made, k + 1)
                        nc.scalar.activation(x1_hi[:, k, :], tmp[:, k % 2, :], ACT.Copy).then_inc(hn_hi, 1)
            mem_source(2 * HEADS_C)
            act.wait_ge(wmod_used, 3 * KT)
            act.wait_ge(w_used, 4 * FIRST["forget"])
            act.dma_start(dist_a[:, :], dist_in).then_inc(dist_loaded, 16)
            for s in range(4):
                split_hi(act, At(4 * FIRST["forget"] + s))
            act.drain().then_inc(turned_copied, 1)
            windows(act, act_window)

            g, r = FIRST["gated"], RESULT["gated"]

            def gated_beat(n, b):
                t = (n.times(4) + (g + b)).times(4)
                for s in range(4):
                    split_hi(act, t + s)
                    if s == 0 and b > 0:
                        act_gate(act, n.times(6) + (r + b - 1), t, b - 1, n)
                    if n.i is None and n.c == 0 and b == 2:
                        if s == 0:
                            act.wait_ge(ctx_free, HEADS_A // 2 + HEADS_B // 2 + HEADS_C + ONE)
                        for k in range(4 * s, 4 * s + 4):
                            nc.scalar.activation(x2_hi[:, k, :], x3[:, k, :], ACT.Copy).then_inc(yz_hi, 1)
                    if n.i is None and n.c == KT - 1 and b == 3:
                        if s == 0:
                            act.wait_ge(y_ready, KT - 1)
                        for k in range(4 * s, min(4 * s + 4, KT - 1)):
                            nc.scalar.activation(x1_hi[:, k, :], x3[:, k, :], ACT.Copy).then_inc(y_hi, 1)
            for b in (2, 3):
                gated_beat(At(0), b)
            with steps(act, 1, KT - 1) as i:
                for b in range(4):
                    gated_beat(At(0, 1, i), b)
            for b in range(4):
                gated_beat(At(KT - 1), b)
            act.wait_ge(y_ready, KT)
            nc.scalar.activation(x1_hi[:, KT - 1, :], x3[:, KT - 1, :], ACT.Copy).then_inc(y_hi, 1)

            def store_result(n):
                act.wait_ge(result_ready, (n + 1).value())
                act.dma_start(out[n.times(P).pick(P), :], result[:, n.parity(), :]).then_inc(result_stored[n.parity()], 16)

            def out_beat(n, peeled=False):
                for s in range(4):
                    split_hi(act, (n + FIRST["out"]).times(4) + s)
                    if s == 1 and not peeled:
                        store_result(n - 1)
            out_beat(At(0), peeled=True)
            out_beat(At(1))
            with steps(act, 1, KT // 2 - 1) as i:
                for slot in range(2):
                    out_beat(At(slot, 2, i))
            out_beat(At(KT - 2))
            out_beat(At(KT - 1))
            store_result(At(KT - 1))
            for n in range(2):
                act.wait_ge(result_stored[n], 16 * KT // 2 + ONE)

        @block.vector
        def _(dve):
            for one in from_one:
                dve.drain().then_inc(one, 1)
            dve.wait_ge(consts_loaded, 16 * 5)
            dve.wait_ge(mask_loaded, 16)
            dve.wait_ge(cols_loaded, 16)
            nc.vector.tensor_copy(ident_b[:, :], ident[:, :])
            nc.vector.tensor_copy(causal_b[:, :], tmp[:, 1, :P])
            nc.vector.tensor_tensor(hn_g[:, :], col("final_g"), col("norm_g"), ALU.mult)
            for name, width in (("qg_a", HEAD), ("qg_b", HEAD), ("qg_c", P)):
                nc.vector.tensor_scalar(col(name), col(name), width ** -0.5, None, ALU.mult)
            dve.drain()

            def variance(source, width, features):
                nc.vector.tensor_scalar(var[:, :width], source, 1.0 / features, EPS, ALU.mult, ALU.add).then_inc(var_ready, 1)

            def mod_column(m):
                slot, k = m % 4, m // 2
                dve.wait_ge(wmod_loaded[slot], 16 * (m // 4 + 1))
                nc.vector.memset(arrived[:, slot:slot + 1], 0.0)
                nc.vector.tensor_tensor_reduce(out=wmod_sb[slot][:, :], in0=wmod_sb[slot][:, :],
                                               in1=c_rows[:, :], scale=1.0, scalar=0.0,
                                               op0=ALU.mult, op1=ALU.add, accum_out=mod_part[:, slot:slot + 1]).then_inc(wmod_used, 1)
                dve.drain()
                if m % 2 == 0:
                    nc.vector.tensor_tensor(mod[:, k:k + 1], mod_part[:, slot:slot + 1], col("b_mod", k), ALU.add)
                else:
                    nc.vector.scalar_tensor_tensor(mod[:, KT + k:KT + k + 1], mod_part[:, slot:slot + 1], 1.0,
                                                   col("b_mod", k + KT), ALU.add, ALU.add)

            r_x = tmp[:, 1, :]
            dve.wait_ge(c_ready, 1)
            for m in range(8):
                mod_column(m)
                if m == 5:
                    dve.wait_ge(square_used, KT)
                    variance(score[1][:, :], T, D)
            rstd_newton(dve, r_x, T, At(0))
            dve.drain().then_inc(rx_ready, 1)
            for j in range(4):
                dve.drain()
                for k in range(4 * j, 4 * j + 4):
                    dve.wait_ge(xr_ready, k + 1)
                    nc.vector.tensor_scalar(h_raw[:, k % 4, :], x3[:, k, :], mod[:, KT + k:KT + k + 1], mod[:, k:k + 1],
                                            ALU.mult, ALU.add).then_inc(h_made, 1)
                dve.drain()
                for k in range(4 * j, 4 * j + 4):
                    dve.wait_ge(h_hi, k + 1)
                    nc.vector.tensor_tensor(x1_lo[:, k, :], h_raw[:, k % 4, :], x1_hi[:, k, :].bitcast(F32),
                                            ALU.subtract).then_inc(h_ready, 1)
                for s in range(8):
                    if 8 * j + s + 3 == 4 * FRONT:
                        dve.wait_ge(lo_ready, 4 * FRONT)
                    if 8 * j + s + 3 >= 4 * FRONT:
                        split_lo(dve, At(8 * j + s))
                    if j < 3:
                        mod_column(8 * (j + 1) + s)

            nc.vector.memset(urow[:, :PAD], 0.0)
            nc.vector.memset(urow[:, PAD + T:], 0.0)
            dve.drain().then_inc(urow_zeroed, 1)

            def silu_of_g(n, source, ring=True):
                dve.wait_ge(sig_ready, (n + 1).value())
                nc.vector.tensor_tensor(tile(x3, n), source[:, :], sig0[:, :], ALU.mult).then_inc(sig_used, 1)
                if ring:
                    dve.drain().then_inc(acc_free[1], 1)

            def ends(row, at):
                return row[:, at:at + T].rearrange("p (a b) -> p a b", b=PAD)[:, 0:T // PAD:T // PAD - 1, :]

            def window_sums(n, grp):
                dve.wait_ge(urow_ready, (n + 1).value())
                level = POOL_WINDOWS[grp].bit_length() - 1
                source = urow
                for j in range(level):
                    width = ROW - (1 << (j + 1)) + 1
                    nc.vector.tensor_tensor(wsum[j % 2][:, :width], source[:, :width],
                                            source[:, 1 << j:(1 << j) + width], ALU.add)
                    dve.drain()
                    source = wsum[j % 2]

            def window_mean(n, grp):
                window = POOL_WINDOWS[grp]
                total = wsum[(window.bit_length() - 2) % 2]
                at = PAD - window // 2
                nc.vector.scalar_tensor_tensor(tmp[:, 0, :], total[:, at:at + T], 1.0 / window,
                                               urow[:, PAD:PAD + T], ALU.mult, ALU.subtract)
                dve.drain()
                table = edges[:, grp, :].rearrange("p (a b) -> p a b", b=PAD)
                nc.vector.tensor_tensor(ends(tmp[:, 0, :], 0), ends(total, at), table, ALU.mult)
                dve.drain()
                nc.vector.tensor_tensor(ends(tmp[:, 0, :], 0), ends(tmp[:, 0, :], 0), ends(urow, PAD),
                                        ALU.subtract).then_inc(urow_used, 1)

            def split_pooled(n):
                split_act(dve, tmp[:, 0, :], tile(x2_hi, n), tile(x2_lo, n), pooled_ready)

            def pool_in_beats(n, grp, peeled=None):
                t = (n.times(2) + FIRST["pool_in"]).times(4)
                for s in range(8):
                    split_lo(dve, t + s)
                    if peeled == 0 and s % 2 == 0:
                        dve.drain()
                        window_sums(At(s // 2), 0)
                        window_mean(At(s // 2), 0)
                    if peeled == 0 and s % 2 == 1:
                        silu_of_g(At(s // 2), bank[s], ring=s == 1)
                        split_pooled(At(s // 2))
                    if peeled == 1 and s == 0:
                        window_sums(n - 1, 1)
                        window_mean(n - 1, 1)
                    if peeled == 1 and s == 2:
                        split_pooled(n - 1)
                    if peeled != 0 and s == 1:
                        silu_of_g(n - 1, acc[1])
                    if peeled != 0 and s == 5:
                        window_sums(n, grp)
                    if peeled != 0 and s == 6:
                        window_mean(n, grp)
                    if peeled != 0 and s == 7:
                        split_pooled(n)
            pool_in_beats(At(4), 1, peeled=0)
            pool_in_beats(At(5), 1, peeled=1)
            for grp in range(1, 4):
                with steps(dve, max(4 * grp, 6), 4 * grp + 4) as i:
                    pool_in_beats(At(0, 1, i), grp)

            def grouped(n):
                r = At(RESULT["group"] + n)
                dve.wait_ge(w_used, 4 * FIRST["group"] + n + 1)
                nc.vector.scalar_tensor_tensor(tmp[:, 0, :], acc[r.parity()][:, :], col("pool_scale", n), x3[:, n, :],
                                               ALU.mult, ALU.mult)
                dve.drain().then_inc(acc_free[r.parity()], 1)
                split_act(dve, tmp[:, 0, :], x1_hi[:, n, :], x1_lo[:, n, :], yg_ready)
            for n in range(KT):
                split_lo(dve, At(4 * FIRST["group"] + n))
                if n == 0:
                    silu_of_g(At(KT - 1), acc[1])
                else:
                    grouped(n - 1)

            def residual(m):
                r = m + RESULT["pool_out"]
                dve.wait_ge(w_used, (m + FIRST["pool_out"] + 1).times(4).value())
                dve.wait_ge(x_in_loaded[m.parity()], ((m.half() + 1).times(16)).value())
                nc.vector.scalar_tensor_tensor(tile(x3, m), acc[r.parity()][:, :], mod[:, (m + 2 * KT).pick()],
                                               x_in[:, m.parity(), :], ALU.mult, ALU.add).then_inc(x1_ready, 1)
                dve.drain().then_inc(acc_free[r.parity()], 1)

            def pool_out_beat(m, peeled=False):
                for s in range(4):
                    split_lo(dve, (m + FIRST["pool_out"]).times(4) + s)
                    if s == 0:
                        if peeled:
                            grouped(KT - 1)
                        else:
                            residual(m - 1)
                    if s == 2:
                        slot = m.parity()
                        if peeled:
                            dve.wait_ge(c_ready, 2)
                        dve.wait_ge(wmod_loaded[slot], ((m.half() + (KT // 2 + 1)).times(16)).value())
                        nc.vector.memset(arrived[:, slot:slot + 1], 0.0)
                        nc.vector.tensor_tensor_reduce(
                            out=wmod_sb[slot][:, :], in0=wmod_sb[slot][:, :], in1=c_rows3[:, :], scale=1.0, scalar=0.0,
                            op0=ALU.mult, op1=ALU.add, accum_out=mod_part[:, slot:slot + 1]).then_inc(wmod_used, 1)
                        dve.drain()
                        k = m + 2 * KT
                        nc.vector.tensor_tensor(mod[:, k.pick()], mod_part[:, slot:slot + 1], col("b_mod", k), ALU.add)
                        dve.drain()
            def normalised_memory(k):
                nc.vector.scalar_tensor_tensor(tmp[:, 1, :MEM], tile(mem_raw, k), col("mem_g", k), r_mem[:, :],
                                               ALU.mult, ALU.mult)
                split_act(dve, tmp[:, 1, :MEM], tile(memn_hi, k), tile(memn_lo, k), memn_ready)

            for m in range(4):
                pool_out_beat(At(m), peeled=m == 0)
                if m == 2:
                    dve.wait_ge(mem_sum_full, 1)
                    variance(score[0][:, :MEM], MEM, D)
                if m == 3:
                    rstd_newton(dve, r_mem[:, :], MEM, At(1))
            with steps(dve, 2, 6) as i:
                for slot in range(2):
                    pool_out_beat(At(slot, 2, i))
                    for n in range(2):
                        normalised_memory(At(2 * slot + n - 8, 4, i))
            with steps(dve, 6, KT // 2) as i:
                for slot in range(2):
                    pool_out_beat(At(slot, 2, i))

            def mem_finish(n, s):
                kind, before = mem_kind(n), (n - 1) % 2
                if s == 2:
                    dve.wait_ge(misc_full, n + ONE)
                    if kind == "k":
                        variance(misc[:, :MEM], MEM, P)
                    else:
                        dve.wait_ge(mem_out_stored, 16 * (n - 1))
                        nc.vector.tensor_copy(mem_out[:, :], misc[:, :MEM]).then_inc(mem_out_ready, 1)
                    dve.drain().then_inc(misc_free, 1)
                if s == 3 and kind == "k":
                    rstd_newton(dve, rs[:, :MEM], MEM, At(2 if n == 1 else n + 3))
                    if n > 1:
                        dve.wait_ge(mem_out_stored, 16 * (n - 1))
                    nc.vector.scalar_tensor_tensor(mem_out[:, :], acc[before][:, :MEM], col("kg_c"), rs[:, :MEM],
                                                   ALU.mult, ALU.mult).then_inc(mem_out_ready, 1)
                    dve.drain().then_inc(acc_free[before], 1)

            def hn_low(k):
                dve.wait_ge(hn_hi, k + 1)
                nc.vector.tensor_tensor(x1_lo[:, k, :], tmp[:, k % 2, :], x1_hi[:, k, :].bitcast(F32),
                                        ALU.subtract).then_inc(hn_ready, 1)

            for n in range(2 * HEADS_C):
                for s in range(4):
                    split_lo(dve, At(4 * (FIRST["mem"] + n) + s))
                    if n == 0 and s == 0:
                        residual(At(KT - 1))
                    if n > 0:
                        mem_finish(n, s)
                    if n == 1 and s == 3:
                        dve.wait_ge(sums_full, 1)
                        variance(score[0][:, :], T, D)
                    if n == 2 and s == 0:
                        rstd_newton(dve, r_one[:, :], T, At(3))
                        dve.wait_ge(sums_full, 2)
                        nc.vector.scalar_tensor_tensor(var[:, :], score[1][:, :], 1.0 / D, r_one[:, :], ALU.mult, ALU.mult)
                        dve.drain().then_inc(score_read, 1)
                        nc.vector.tensor_tensor(var[:, :], var[:, :], r_one[:, :], ALU.mult)
                        dve.drain()
                        nc.vector.tensor_scalar(var[:, :], var[:, :], EPS, None, ALU.add).then_inc(var_ready, 1)
                    if n == 2 and s == 1:
                        rstd_newton(dve, rs[:, :], T, At(4))
                        nc.vector.tensor_tensor(r_both[:, :], rs[:, :], r_one[:, :], ALU.mult)
                    if 3 <= n < 7:
                        k = 4 * (n - 3) + s
                        nc.vector.scalar_tensor_tensor(tmp[:, k % 2, :], x3[:, k, :], hn_g[:, k:k + 1], r_both[:, :],
                                                       ALU.mult, ALU.mult).then_inc(hn_made, 1)
                        if k > 0:
                            hn_low(k - 1)
                    if n == 7 and s == 0:
                        hn_low(KT - 1)
            mem_finish(2 * HEADS_C, 2)
            for s in range(4):
                split_lo(dve, At(4 * FIRST["forget"] + s))
            dve.drain()
            dve.wait_ge(dist_loaded, 16)
            nc.vector.memset(zero_c[:, :], 0.0)

            def x_prime(k):
                dve.wait_ge(xp_stored[k % 2], 16 * (k // 2))
                nc.vector.scalar_tensor_tensor(tmp[:, k % 2, :], x3[:, k, :], col("final_g", k), r_one[:, :],
                                               ALU.mult, ALU.mult).then_inc(xp_ready, 1)
            windows(dve, dve_window, x_prime)

            g, r = FIRST["gated"], RESULT["gated"]

            def branch(n, b):
                t = (n.times(4) + (g + 3)).times(4)
                dve.wait_ge(w_used, (t + (b + 2)).value())
                dve.wait_ge(gsig_ready, (n.times(3) + (b + 1)).value())
                bank_n = (n.times(6) + (r + 3 + b)).parity()
                nc.vector.tensor_tensor(part[:, min(b, 1), :], acc[bank_n][:, :], gate_sig[:, b, :], ALU.mult)
                dve.drain().then_inc(acc_free[bank_n], 1)
                if b == 1:
                    nc.vector.tensor_tensor(part[:, 0, :], part[:, 0, :], part[:, 1, :], ALU.add)
                    dve.drain()
                if b == 2:
                    nc.vector.tensor_tensor(tile(x3, n), part[:, 0, :], part[:, 1, :], ALU.add).then_inc(y_ready, 1)

            def gated_beat(n, b, peeled=False):
                t = (n.times(4) + (g + b)).times(4)
                for s in range(4):
                    split_lo(dve, t + s)
                    if s == 0 and b == 0:
                        branch(n - 1, 2)
                    if peeled and b == 2:
                        for k in range(4 * s, 4 * s + 4):
                            low_part(k, x2_hi, x2_lo, yz_hi, yz_ready)
                    if b == 3 and s >= 2:
                        branch(n, s - 2)
                    if n.i is None and n.c == KT - 1 and b == 3:
                        for k in range(4 * s, min(4 * s + 4, KT - 1)):
                            low_part(k, x1_hi, x1_lo, y_hi, y_split)

            def low_part(k, hi, lo, hi_done, ready):
                dve.wait_ge(hi_done, k + 1)
                nc.vector.tensor_tensor(lo[:, k, :], x3[:, k, :], hi[:, k, :].bitcast(F32), ALU.subtract).then_inc(ready, 1)

            for b in (2, 3):
                gated_beat(At(0), b, peeled=True)
            with steps(dve, 1, KT - 1) as i:
                for b in range(4):
                    gated_beat(At(0, 1, i), b)
            for b in range(4):
                gated_beat(At(KT - 1), b)
            branch(At(KT - 1), 2)
            dve.drain()
            low_part(KT - 1, x1_hi, x1_lo, y_hi, y_split)

            def finish(n):
                rr = n + RESULT["out"]
                dve.wait_ge(w_used, (n + FIRST["out"] + 1).times(4).value())
                dve.wait_ge(x_back_loaded[n.parity()], ((n.half() + 1).times(16)).value())
                dve.wait_ge(result_stored[n.parity()], (n.half().times(16) + ONE).value())
                nc.vector.tensor_tensor(result[:, n.parity(), :], acc[rr.parity()][:, :], x_back[:, n.parity(), :],
                                        ALU.add).then_inc(result_ready, 1)
                dve.drain().then_inc(acc_free[rr.parity()], 1)

            def out_beat(n, peeled=False):
                for s in range(4):
                    split_lo(dve, (n + FIRST["out"]).times(4) + s)
                    if s == 0 and not peeled:
                        finish(n - 1)
            out_beat(At(0), peeled=True)
            out_beat(At(1))
            with steps(dve, 1, KT // 2 - 1) as i:
                for slot in range(2):
                    out_beat(At(slot, 2, i))
            out_beat(At(KT - 2))
            out_beat(At(KT - 1))
            finish(At(KT - 1))

        @block.gpsimd
        def _(pool):
            pool.wait_ge(rx_ready, 1)
            def rows(j):
                for k in range(4 * j, 4 * j + 4):
                    nc.gpsimd.tensor_tensor(x3[:, k, :], x3[:, k, :], tmp[:, 1, :], ALU.mult).then_inc(xr_ready, 1)

            def front_lo(s):
                pool.wait_ge(hi_ready, s + 1)
                nc.gpsimd.tensor_tensor(w_lo[:, s % 4, :], raw_quarter(At(s)), w_hi[:, s % 4, :].bitcast(F32),
                                        ALU.subtract).then_inc(lo_ready, 1)
            rows(0)
            for s in range(3):
                front_lo(s)
            for j in range(4):
                if j < 3:
                    rows(j + 1)
                for s in range(8 * j + 3, min(8 * j + 11, 4 * FRONT)):
                    front_lo(s)
            pool.wait_ge(sig_used, KT + ONE)
            for total in (sum_a, sum_b):
                nc.gpsimd.memset(total[:, :], 0.0).then_inc(sums_zeroed, 1)
            pool.wait_ge(sums_zeroed, 2)
            with steps(pool, 0, KT) as i:
                for which, (total, square) in enumerate(((sum_a, sq_a), (sum_b, sq_b))):
                    pool.wait_ge(sq_ready, At(which + 1, 2, i).value())
                    pool.wait_ge(sq_added, (At(which, 2, i) + ONE).value())
                    nc.gpsimd.tensor_tensor(total[:, :], total[:, :], square[:, :], ALU.add).then_inc(sq_added, 1)
            with steps(pool, 0, 2 * HEADS_C) as i:
                n = At(0, 1, i)
                pool.wait_ge(mem_out_ready, (n + 1).value())
                pool.dma_start(mkv_store[n.pick(), :, :].rearrange("a p t -> p (a t)"), mem_out[:, :]).then_inc(mem_out_stored, 16)
            with steps(pool, 0, KT // 2) as i:
                for slot in range(2):
                    k = At(slot, 2, i)
                    pool.wait_ge(xp_ready, (k + 1).value())
                    pool.dma_start(x_store[k.pick(), :, :].rearrange("a p t -> p (a t)"), tmp[:, slot, :]).then_inc(xp_stored[slot], 16)
            pool.wait_ge(c_neg_ready, 1)
            pool.dma_start(c_store, f_a[:HEADS_B, :]).then_inc(c_stored, 16)
            pool.wait_ge(c_stored, 16)
            windows(pool, pool_window)


def panels(w):
    k, n = w.shape
    return w.reshape(k // P, P, n // P, P).transpose(2, 1, 0, 3).reshape(n // P, P, k)


def weight_stream(inputs):
    w_in = inputs["w_in_2"][0]
    sizes = [HEADS_A * HEAD, HEADS_A * HEAD // GROUPS, HEADS_A * HEAD // GROUPS, HEADS_A * HEAD] + \
        [HEADS_B * HEAD] * 4 + [HEADS_B, HEADS_C * P, HEADS_C * P, 3 * D]
    qa, ka, va, za, qb, kb, vb, zb, fb, qc, zc, gates = np.split(w_in, np.cumsum(sizes)[:-1], axis=1)
    order = np.concatenate([np.arange(HEAD * h, HEAD * h + HEAD) for h in a_heads()])
    qa, za = panels(qa[:, order]), panels(za[:, order])
    ka, va = panels(ka), panels(va)
    qb, kb, vb, zb, qc, zc = (panels(w) for w in (qb, kb, vb, zb, qc, zc))
    mem = panels(inputs["w_mem_kv_2"][0])
    pool_in = panels(inputs["pool_w_in"][0])
    grouped = []
    for w in inputs["pool_w_grp"][0]:
        grouped.append(panels(w).transpose(1, 0, 2).reshape(1, P, 4 * w.shape[0]))
    forget = np.zeros((D, P), np.float32)
    forget[:, :HEADS_B] = fb
    gates = [panels(g) for g in np.split(gates, 3, axis=1)]
    branch = panels(np.concatenate([inputs["w_branch_a_2"][0][order], inputs["w_branch_b_2"][0],
                                    inputs["w_branch_c_2"][0]]))
    pool_out, w_out = panels(inputs["pool_w_out"][0]), panels(inputs["w_out_2"][0])

    def mixed(*parts):
        return np.stack(parts, axis=1).reshape(-1, P, D)
    a = []
    for c in range(2):
        a += [ka[c:c + 1], va[c:c + 1]]
        for g in range(GROUPS):
            j = GROUPS * c + g
            a += [qa[j:j + 1], za[j:j + 1]]
    u_and_g = mixed(pool_in[:KT], pool_in[KT:])
    front = u_and_g[:FRONT].reshape(2, 4, P, 4, 4 * P).transpose(3, 0, 2, 1, 4).reshape(FRONT, P, D)
    return np.ascontiguousarray(np.concatenate(
        [front, u_and_g[FRONT:], *grouped, pool_out, mem, panels(forget), mixed(kb, vb, qb, zb), *a,
         mixed(qc, zc), mixed(*gates, branch), w_out]))


def small_columns(inputs):
    def tiles(v):
        return v.reshape(-1, P).T
    forget = np.zeros((P, 1), np.float32)
    forget[:HEADS_B, 0] = inputs["b_forget_2"][0]

    def twice(name):
        return np.tile(inputs[name][0], 2).reshape(P, 1)
    sinks = np.broadcast_to(inputs["sinks_a_2"][0][a_heads()], (P, HEADS_A))
    return np.ascontiguousarray(np.concatenate(
        [tiles(inputs["b_mod"][0]), tiles(inputs["pool_scale"][0]), tiles(inputs["final_norm_g"]),
         tiles(inputs["norm_gain_2"][0]), tiles(inputs["mem_norm_gain_2"][0]), forget,
         twice("q_gain_a_2"), twice("k_gain_a_2"), twice("q_gain_b_2"), twice("k_gain_b_2"),
         inputs["q_gain_c_2"][0].reshape(P, 1), inputs["k_gain_c_2"][0].reshape(P, 1), sinks], axis=1))


def shape_constants():
    edge = np.zeros((4, 2 * PAD), np.float32)
    for j, w in enumerate(POOL_WINDOWS):
        for e, t in enumerate([*range(PAD), *range(T - PAD, T)]):
            edge[j, e] = 1.0 / (min(t + w // 2, T) - max(t - w // 2, 0))
    p = np.arange(P)
    slopes = 2.0 ** (-8.0 * (np.array(a_heads()) + 1) / HEADS_A)
    full = np.concatenate(
        [np.eye(P), np.ones((P, P)), (p[:, None] // HEAD == p[None, :] // HEAD).astype(float),
         np.where(p[None, :] > p[:, None], NEG, 0.0), np.broadcast_to(edge.reshape(1, -1), (P, edge.size)),
         np.broadcast_to(slopes, (P, HEADS_A))], axis=1).astype(np.float32)
    back = p[:, None] + P - np.arange(2 * P)[None, :]
    dist = np.where((back >= 0) & (back < P), -back, FAR).astype(np.float32)
    return full, dist


def kernel(**inputs):
    import concourse.bacc as bacc
    from concourse.bass_utils import run_bass_kernel_spmd

    inputs = {name: np.asarray(value) for name, value in inputs.items()}
    full, dist = shape_constants()
    arrays = {
        "stream": weight_stream(inputs),
        "w_mod_rows": np.ascontiguousarray(inputs["w_mod"][0].T),
        "c_row": np.ascontiguousarray(inputs["c"]),
        "x_features": np.ascontiguousarray(inputs["x"][0].T),
        "mem_features": np.ascontiguousarray(inputs["mem_2"][0].T),
        "columns": small_columns(inputs),
        "constants": full,
        "distances": dist,
    }
    nc = bacc.Bacc("TRN2", target_bir_lowering=False, num_devices=1)
    aps = [nc.dram_tensor(name, a.shape, F32, kind="ExternalInput").ap() for name, a in arrays.items()]
    stores = [nc.dram_tensor(name, shape, F32, kind="Internal").ap() for name, shape in
              (("x_store", (KT, P, T)), ("c_store", (HEADS_B, T)), ("mkv_store", (2 * HEADS_C, P, MEM)))]
    result = nc.dram_tensor("result_features", (D, T), F32, kind="ExternalOutput").ap()
    program(nc, *aps, *stores, result)
    got = run_bass_kernel_spmd(nc, [arrays], core_ids=[0])
    return np.ascontiguousarray(got.results[0]["result_features"].T).reshape(1, T, D)
```
